# Optimizing a Trainium2 kernel written in Bass

```python
import jax
import jax.numpy as jnp
from jax import lax
import numpy as np

D_MODEL = 1024
BATCH = 1
SEQ = 256
DEPTH = 2

GDN_HEADS = 4
GDN_HEAD_DIM = 128
GDN_WIDTH = GDN_HEADS * GDN_HEAD_DIM
GDN_CONV = 4
GDN_CHUNK = 64
RWKV_HEADS = 8
RWKV_HEAD_DIM = 64
RWKV_WIDTH = RWKV_HEADS * RWKV_HEAD_DIM
RWKV_W_LORA = 64
RWKV_A_LORA = 64
RWKV_G_LORA = 128
RWKV_IN = 3 * RWKV_WIDTH + RWKV_W_LORA + RWKV_A_LORA + RWKV_G_LORA
SB_HEADS = 8
SB_HEAD_DIM = 64
SB_WIDTH = SB_HEADS * SB_HEAD_DIM
SB_BLOCK = 128
N_BRANCH = 3
IN_SPLITS = (3 * GDN_WIDTH, GDN_WIDTH, GDN_HEADS, GDN_HEADS, RWKV_IN, 3 * SB_WIDTH, N_BRANCH * D_MODEL)
D_IN = 3 * GDN_WIDTH + GDN_WIDTH + 2 * GDN_HEADS + RWKV_IN + 3 * SB_WIDTH + N_BRANCH * D_MODEL
D_FF_DENSE = 2816
N_EXPERTS = 8
TOP_K = 2
D_FF_EXPERT = 3584
N_DENSE_LAYERS = (DEPTH + 1) // 2
N_MOE_LAYERS = DEPTH // 2
RMS_EPS = 1e-6
GN_EPS = 64e-5
L2_EPS = 1e-6

kernel_name = "hybrid_gdn_rwkv7_stickbreak_moe"

def _split(h, sizes):
    out, start = [], 0
    for s in sizes:
        out.append(h[..., start:start + s])
        start += s
    return out

def rmsnorm(x, g):
    xf = x.astype(jnp.float32)
    y = xf * lax.rsqrt(jnp.mean(xf * xf, axis=-1, keepdims=True) + RMS_EPS)
    return (y * g.astype(jnp.float32)).astype(x.dtype)

def l2norm(x):
    return x * lax.rsqrt(jnp.sum(x * x, axis=-1, keepdims=True) + L2_EPS)

def causal_shift(h):
    return jnp.pad(h, ((0, 0), (1, 0), (0, 0)))[:, :-1]

def causal_short_conv(h, w):
    T = h.shape[1]
    K = w.shape[0]
    hp = jnp.pad(h, ((0, 0), (K - 1, 0), (0, 0)))
    y = hp[:, 0:T] * w[0]
    for i in range(1, K):
        y = y + hp[:, i:i + T] * w[i]
    return jax.nn.silu(y)

def gated_delta_rule_chunked(q, k, v, g, beta):
    B_, H, T, Dk = q.shape
    Dv = v.shape[-1]
    C = GDN_CHUNK
    N = T // C
    q = q.reshape(B_, H, N, C, Dk)
    k = k.reshape(B_, H, N, C, Dk)
    v = v.reshape(B_, H, N, C, Dv)
    beta = beta.reshape(B_, H, N, C)
    g = jnp.cumsum(g.reshape(B_, H, N, C), axis=-1)
    tri_incl = jnp.tril(jnp.ones((C, C), dtype=bool))
    tri_strict = jnp.tril(jnp.ones((C, C), dtype=bool), -1)
    decay = jnp.exp(jnp.where(tri_incl, g[..., :, None] - g[..., None, :], -jnp.inf))
    k_beta = k * beta[..., None]
    v_beta = v * beta[..., None]
    m = jnp.where(tri_strict, jnp.einsum('bhnid,bhnjd->bhnij', k_beta, k) * decay, 0.0)
    eye = jnp.eye(C, dtype=q.dtype)
    rhs = jnp.concatenate([v_beta, k_beta * jnp.exp(g)[..., None]], axis=-1)
    sol = lax.linalg.triangular_solve(eye + m, rhs, left_side=True, lower=True, unit_diagonal=True)
    u, w = sol[..., :Dv], sol[..., Dv:]
    attn = jnp.where(tri_incl, jnp.einsum('bhnid,bhnjd->bhnij', q, k) * decay, 0.0)
    g_last = g[..., -1]
    q_dec = q * jnp.exp(g)[..., None]
    k_dec = k * jnp.exp(g_last[..., None] - g)[..., None]
    xs = tuple(jnp.moveaxis(t, 2, 0) for t in (q_dec, k_dec, u, w, attn, g_last))

    def step(S, inp):
        qd, kd, u_c, w_c, a_c, gl = inp
        v_new = u_c - jnp.einsum('bhck,bhkv->bhcv', w_c, S)
        o = jnp.einsum('bhck,bhkv->bhcv', qd, S) + jnp.einsum('bhij,bhjv->bhiv', a_c, v_new)
        S = S * jnp.exp(gl)[..., None, None] + jnp.einsum('bhck,bhcv->bhkv', kd, v_new)
        return S, o

    S0 = jnp.zeros((B_, H, Dk, Dv), q.dtype)
    _, o = lax.scan(step, S0, xs)
    return jnp.moveaxis(o, 0, 2).reshape(B_, H, T, Dv)

def gated_deltanet(h_qkv, h_z, h_b, h_a, conv_w, a_log, dt_bias, norm_g):
    B_, T, _ = h_qkv.shape
    qkv = causal_short_conv(h_qkv, conv_w).astype(jnp.float32)
    q, k, v = jnp.split(qkv, 3, axis=-1)

    def heads(t):
        return t.reshape(B_, T, GDN_HEADS, GDN_HEAD_DIM).transpose(0, 2, 1, 3)

    q = l2norm(heads(q)) * (GDN_HEAD_DIM ** -0.5)
    k = l2norm(heads(k))
    v = heads(v)
    beta = jax.nn.sigmoid(h_b.astype(jnp.float32)).transpose(0, 2, 1)
    g = -jnp.exp(a_log.astype(jnp.float32)) * jax.nn.softplus(
        h_a.astype(jnp.float32) + dt_bias.astype(jnp.float32))
    g = g.transpose(0, 2, 1)
    o = gated_delta_rule_chunked(q, k, v, g, beta).transpose(0, 2, 1, 3)
    o = o * lax.rsqrt(jnp.mean(o * o, axis=-1, keepdims=True) + RMS_EPS) * norm_g.astype(jnp.float32)
    z = h_z.astype(jnp.float32).reshape(B_, T, GDN_HEADS, GDN_HEAD_DIM)
    o = o * jax.nn.silu(z)
    return o.reshape(B_, T, GDN_WIDTH).astype(h_qkv.dtype)

def rwkv7_time_mix(h, mu, w0, w2, a0, a2, g2, k_k, k_a, r_k, ln_g, ln_b):
    B_, T, _ = h.shape
    hf = h.astype(jnp.float32)
    hl = hf + (causal_shift(hf) - hf) * mu.astype(jnp.float32)
    r, k, v, xw, xa, xg = _split(hl, (RWKV_WIDTH, RWKV_WIDTH, RWKV_WIDTH, RWKV_W_LORA, RWKV_A_LORA, RWKV_G_LORA))
    w_log = -jax.nn.softplus(-(w0 + jnp.tanh(xw) @ w2)) - 0.5
    decay = jnp.exp(-jnp.exp(w_log))
    a = jax.nn.sigmoid(a0 + xa @ a2)
    gate = jax.nn.sigmoid(xg) @ g2
    kk = k * k_k
    k = k * (1.0 + (a - 1.0) * k_a)

    def heads(t):
        return t.reshape(B_, T, RWKV_HEADS, RWKV_HEAD_DIM)

    r_h, w_h, k_h, v_h, a_h = heads(r), heads(decay), heads(k), heads(v), heads(a)
    kk_h = l2norm(heads(kk))
    xs = tuple(t.transpose(1, 0, 2, 3) for t in (r_h, w_h, k_h, v_h, kk_h, a_h))

    def step(S, inp):
        r_t, w_t, k_t, v_t, kk_t, a_t = inp
        sa = jnp.einsum('bhvk,bhk->bhv', S, kk_t)
        S = (S * w_t[:, :, None, :]
             - sa[..., None] * (kk_t * a_t)[:, :, None, :]
             + v_t[..., None] * k_t[:, :, None, :])
        y = jnp.einsum('bhvk,bhk->bhv', S, r_t)
        return S, y

    S0 = jnp.zeros((B_, RWKV_HEADS, RWKV_HEAD_DIM, RWKV_HEAD_DIM), jnp.float32)
    _, y = lax.scan(step, S0, xs)
    y = y.transpose(1, 0, 2, 3)
    mean = jnp.mean(y, axis=-1, keepdims=True)
    var = jnp.mean(jnp.square(y - mean), axis=-1, keepdims=True)
    y = ((y - mean) * lax.rsqrt(var + GN_EPS)).reshape(B_, T, RWKV_WIDTH) * ln_g + ln_b
    bonus = jnp.sum(r_h * k_h * r_k, axis=-1, keepdims=True) * v_h
    y = (y + bonus.reshape(B_, T, RWKV_WIDTH)) * gate
    return y.astype(h.dtype)

def stick_breaking_attention(h_qkv):
    B_, T, _ = h_qkv.shape
    q, k, v = jnp.split(h_qkv, 3, axis=-1)

    def heads(t):
        return t.reshape(B_, T, SB_HEADS, SB_HEAD_DIM).transpose(0, 2, 1, 3)

    q, k, v = heads(q), heads(k), heads(v)
    scale = SB_HEAD_DIM ** -0.5
    outs = []
    for start in range(0, T, SB_BLOCK):
        end = start + SB_BLOCK
        z = jnp.einsum('bhqd,bhkd->bhqk', q[:, :, start:end], k[:, :, :end]).astype(jnp.float32) * scale
        mask = jnp.arange(end)[None, :] < (start + jnp.arange(SB_BLOCK))[:, None]
        log_1mb = jnp.where(mask, jax.nn.log_sigmoid(-z), 0.0)
        log_a = jax.nn.log_sigmoid(z) + lax.cumsum(log_1mb, axis=3, reverse=True) - log_1mb
        att = jnp.where(mask, jnp.exp(log_a), 0.0).astype(v.dtype)
        outs.append(jnp.einsum('bhqk,bhkd->bhqd', att, v[:, :, :end]))
    o = jnp.concatenate(outs, axis=2)
    return o.transpose(0, 2, 1, 3).reshape(B_, T, SB_WIDTH)

def swiglu(h, w_gate, w_up, w_down):
    return (jax.nn.silu(h @ w_gate) * (h @ w_up)) @ w_down

def moe_swiglu(h, router_w, w_gate, w_up, w_down):
    B_, T, D = h.shape
    tokens = h.reshape(B_ * T, D)
    logits = (tokens @ router_w).astype(jnp.float32)
    top_vals, top_idx = lax.top_k(logits, TOP_K)
    top_w = jax.nn.softmax(top_vals, axis=-1)
    combine = jnp.sum(jax.nn.one_hot(top_idx, N_EXPERTS, dtype=jnp.float32) * top_w[..., None], axis=1)
    out = jnp.zeros_like(tokens)
    for e in range(N_EXPERTS):
        y = swiglu(tokens, w_gate[e], w_up[e], w_down[e])
        out = out + combine[:, e:e + 1].astype(tokens.dtype) * y
    return out.reshape(B_, T, D)

def setup_inputs(seed: int = 0) -> dict:
    key = jax.random.key(seed)
    ks = iter(jax.random.split(key, 48))

    def nrm(shape, scale):
        return jax.random.normal(next(ks), shape, jnp.float32) * scale

    def uni(shape, lo, hi):
        return jax.random.uniform(next(ks), shape, jnp.float32, minval=lo, maxval=hi)

    L = DEPTH
    return {
        "x": nrm((BATCH, SEQ, D_MODEL), 1.0),
        "norm_mix_g": 1.0 + nrm((L, D_MODEL), 0.02),
        "w_in": nrm((L, D_MODEL, D_IN), D_MODEL ** -0.5),
        "gdn_conv_w": nrm((L, GDN_CONV, 3 * GDN_WIDTH), GDN_CONV ** -0.5),
        "gdn_a_log": jnp.log(uni((L, GDN_HEADS), 1.0, 16.0)),
        "gdn_dt_bias": nrm((L, GDN_HEADS), 0.1),
        "gdn_norm_g": 1.0 + nrm((L, GDN_HEAD_DIM), 0.02),
        "rwkv_mu": uni((L, RWKV_IN), 0.0, 1.0),
        "rwkv_w0": uni((L, RWKV_WIDTH), -6.0, -1.0),
        "rwkv_w2": nrm((L, RWKV_W_LORA, RWKV_WIDTH), 0.1 * RWKV_W_LORA ** -0.5),
        "rwkv_a0": nrm((L, RWKV_WIDTH), 0.1),
        "rwkv_a2": nrm((L, RWKV_A_LORA, RWKV_WIDTH), RWKV_A_LORA ** -0.5),
        "rwkv_g2": nrm((L, RWKV_G_LORA, RWKV_WIDTH), RWKV_G_LORA ** -0.5),
        "rwkv_k_k": 0.85 + nrm((L, RWKV_WIDTH), 0.02),
        "rwkv_k_a": 1.0 + nrm((L, RWKV_WIDTH), 0.02),
        "rwkv_r_k": nrm((L, RWKV_HEADS, RWKV_HEAD_DIM), 0.1),
        "rwkv_ln_g": 1.0 + nrm((L, RWKV_WIDTH), 0.02),
        "rwkv_ln_b": nrm((L, RWKV_WIDTH), 0.02),
        "w_branch_gdn": nrm((L, GDN_WIDTH, D_MODEL), GDN_WIDTH ** -0.5),
        "w_branch_rwkv": nrm((L, RWKV_WIDTH, D_MODEL), RWKV_WIDTH ** -0.5),
        "w_branch_sb": nrm((L, SB_WIDTH, D_MODEL), SB_WIDTH ** -0.5),
        "w_out": nrm((L, D_MODEL, D_MODEL), D_MODEL ** -0.5),
        "norm_ffn_g": 1.0 + nrm((L, D_MODEL), 0.02),
        "ffn_w_gate": nrm((N_DENSE_LAYERS, D_MODEL, D_FF_DENSE), D_MODEL ** -0.5),
        "ffn_w_up": nrm((N_DENSE_LAYERS, D_MODEL, D_FF_DENSE), D_MODEL ** -0.5),
        "ffn_w_down": nrm((N_DENSE_LAYERS, D_FF_DENSE, D_MODEL), D_FF_DENSE ** -0.5),
        "router_w": nrm((N_MOE_LAYERS, D_MODEL, N_EXPERTS), D_MODEL ** -0.5),
        "moe_w_gate": nrm((N_MOE_LAYERS, N_EXPERTS, D_MODEL, D_FF_EXPERT), D_MODEL ** -0.5),
        "moe_w_up": nrm((N_MOE_LAYERS, N_EXPERTS, D_MODEL, D_FF_EXPERT), D_MODEL ** -0.5),
        "moe_w_down": nrm((N_MOE_LAYERS, N_EXPERTS, D_FF_EXPERT, D_MODEL), D_FF_EXPERT ** -0.5),
        "final_norm_g": 1.0 + nrm((D_MODEL,), 0.02),
    }

def reference(x, norm_mix_g, w_in, gdn_conv_w, gdn_a_log, gdn_dt_bias, gdn_norm_g,
              rwkv_mu, rwkv_w0, rwkv_w2, rwkv_a0, rwkv_a2, rwkv_g2, rwkv_k_k, rwkv_k_a,
              rwkv_r_k, rwkv_ln_g, rwkv_ln_b, w_branch_gdn, w_branch_rwkv, w_branch_sb,
              w_out, norm_ffn_g, ffn_w_gate, ffn_w_up, ffn_w_down, router_w,
              moe_w_gate, moe_w_up, moe_w_down, final_norm_g):
    B_, T, D = x.shape
    for layer in range(DEPTH):
        hn = rmsnorm(x, norm_mix_g[layer])
        proj = hn @ w_in[layer]
        h_gdn_qkv, h_gdn_z, h_gdn_b, h_gdn_a, h_rwkv, h_sb, h_gate = _split(proj, IN_SPLITS)
        o_a = gated_deltanet(h_gdn_qkv, h_gdn_z, h_gdn_b, h_gdn_a, gdn_conv_w[layer],
                             gdn_a_log[layer], gdn_dt_bias[layer], gdn_norm_g[layer])
        o_b = rwkv7_time_mix(h_rwkv, rwkv_mu[layer], rwkv_w0[layer], rwkv_w2[layer],
                             rwkv_a0[layer], rwkv_a2[layer], rwkv_g2[layer], rwkv_k_k[layer],
                             rwkv_k_a[layer], rwkv_r_k[layer], rwkv_ln_g[layer], rwkv_ln_b[layer])
        o_c = stick_breaking_attention(h_sb)
        gates = jax.nn.sigmoid(h_gate.astype(jnp.float32)).astype(x.dtype).reshape(B_, T, N_BRANCH, D)
        merged = (gates[:, :, 0] * (o_a @ w_branch_gdn[layer])
                  + gates[:, :, 1] * (o_b @ w_branch_rwkv[layer])
                  + gates[:, :, 2] * (o_c @ w_branch_sb[layer]))
        x = x + merged @ w_out[layer]
        hn = rmsnorm(x, norm_ffn_g[layer])
        if layer % 2 == 0:
            i = layer // 2
            x = x + swiglu(hn, ffn_w_gate[i], ffn_w_up[i], ffn_w_down[i])
        else:
            i = layer // 2
            x = x + moe_swiglu(hn, router_w[i], moe_w_gate[i], moe_w_up[i], moe_w_down[i])
    return rmsnorm(x, final_norm_g)


_drawn_inputs = setup_inputs


def setup_inputs(seed=0):
    import zlib

    import numpy as np

    out = dict(_drawn_inputs(seed))
    spreads = {}
    factors = {'gdn_dt_bias': 5.314,
     'rwkv_w2': 8.0,
     'rwkv_k_a': 2.745,
     'rwkv_ln_b': 2.954,
     'final_norm_g': 2.774}
    for name, (base, spread) in spreads.items():
        noise = np.random.default_rng([zlib.crc32(name.encode()), seed]).standard_normal(out[name].shape)
        drawn = base * np.exp(spread * noise) if base else spread * noise
        out[name] = jnp.asarray(drawn.astype(out[name].dtype))
    for name, factor in factors.items():
        out[name] = (out[name] * factor).astype(out[name].dtype)
    return out
```

```python
import math
from contextlib import ExitStack

import concourse.bass as bass
from concourse import mybir

F32 = mybir.dt.float32
I32 = mybir.dt.int32
ALU = mybir.AluOpType
ACT = mybir.ActivationFunctionType
AX_X = mybir.AxisListType.X

P = 128
D = 1024
KD = D // P
T = 256
NT = T // P
C = 64
NCH = T // C
DEPTH = 2
GH = 4
RP = 4
GW = 512
O_Z, O_BA, O_RW, O_SB, O_GATE = 1536, 2048, 2056, 3848, 5384
RW_TILES = 14
FFD, FFE, NE = 2816, 3584, 8
RMS_EPS, L2_EPS, GN_EPS = 1e-6, 1e-6, 64e-5
W_FACTOR = 0.6065306597126334
NEG = -1e30
CAP = P
MAX_PASSES = 2 * T // CAP + NE
SLOT = 2048
RING = 6
MRING = 14
FT = FFE // P
SW = 256

V_NMG, V_NFG, V_CONV, V_MU, V_A0, V_KK, V_KA, V_RK, V_LNG, V_LNB, V_GNG = 0, 8, 16, 64, 78, 82, 86, 90, 94, 98, 102
V_ROWS = 103


class Signal:

    def __init__(self, handle, per_layer):
        self.handle, self.per_layer, self.given = handle, per_layer, 0

    def by(self, ins, n=1):
        self.given += n
        return ins.then_inc(self.handle, n)

    def wait(self, eng, layer, count):
        value = layer * self.per_layer + count
        if value > 0:
            eng.wait_ge(self.handle, value)


def build(nc, a, out):
    ctx = ExitStack()
    with ctx:
        def sb(name, shape, dt=F32):
            return ctx.enter_context(nc.sbuf_tensor(name, shape, dt))

        def sem(name):
            return ctx.enter_context(nc.semaphore(name))

        signals = []

        def sig(name, per_layer):
            s = Signal(sem(name), per_layer)
            signals.append((name, s))
            return s

        x = sb("x", [P, NT, D])
        hn = sb("hn", [P, NT, D])
        hnT = sb("hnT", [P, KD, T])
        oT = sb("oT", [P, 3, GH, T])
        ident = sb("ident", [P, P])
        ones = sb("ones", [P, P])
        same_chunk = sb("same_chunk", [P, P])
        incl = sb("incl", [P, P])
        strict = sb("strict", [P, P])
        before = sb("before", [P, P])
        neg_incl = sb("neg_incl", [P, P])
        neg_strict = sb("neg_strict", [P, P])
        gram_mask = sb("gram_mask", [P, 4, P])
        level_mask = sb("level_mask", [P, 6, P])
        tri_mid = sb("tri_mid", [P, 2 * P + 4])
        neg_suffix = sb("neg_suffix", [P, P])
        neg_ones = sb("neg_ones", [P, P])
        chunk_rows = sb("chunk_rows", [P, 2, P])
        slots_iota = sb("slots_iota", [P, CAP])
        vec_rows = sb("vec_rows", [P, DEPTH, P])
        vecs = sb("vecs", [P, DEPTH, V_ROWS + 1])
        lora = sb("lora", [P, DEPTH, GW])
        g2 = sb("g2", [P, DEPTH, GW])
        w0 = sb("w0", [P, DEPTH, GW])
        head_scalars = sb("head_scalars", [P, DEPTH, 2, GH])
        router_w = sb("router_w", [P, KD, NE])
        eps_c = sb("eps_c", [P, 4])
        stat = sb("stat", [P, 64])
        sc = sb("sc", [P, 176])

        ring_floats = RING * SLOT
        arena_floats = (nc.sbuf_usable_end - nc.sbuf_base) // 4 - ring_floats - 40
        pool = sb("pool", [P, ring_floats + arena_floats])
        top = [ring_floats]

        def region(floats, at=None):
            start = top[0] if at is None else at
            assert start + floats <= ring_floats + arena_floats, (start, floats, ring_floats + arena_floats)
            top[0] = max(top[0], start + floats) if at is None else top[0]
            return pool[:, start:start + floats]

        def slot(n):
            return pool[:, n * SLOT:(n + 1) * SLOT]

        banks = [ctx.enter_context(nc.psum_tensor(f"bank{i}", [P, 512], F32)) for i in range(8)]
        proj, B = banks[:2], banks[2:]

        stage = region(2 * 2 * 260).rearrange("p (b t n) -> p b t n", b=2, t=2)
        X = region(1024).rearrange("p (i n) -> p i n", i=8)
        XT = region(1024).rearrange("p (i n) -> p i n", i=8)
        Y = region(1024).rearrange("p (i n) -> p i n", i=8)
        Ml = region(1024).rearrange("p (i n) -> p i n", i=8)
        shared = top[0]
        qkv = region(12 * T).rearrange("p (j t) -> p j t", j=12)
        zT = region(GH * T).rearrange("p (h t) -> p h t", h=GH)
        kb = region(1024).rearrange("p (t h n) -> p t h n", t=NT, h=GH)
        kdec = region(1024).rearrange("p (t h n) -> p t h n", t=NT, h=GH)
        vb = region(1024).rearrange("p (t h n) -> p t h n", t=NT, h=GH)
        qdec = region(1024).rearrange("p (t h n) -> p t h n", t=NT, h=GH)
        EE = region(2048).rearrange("p (t k h n) -> p t k h n", t=NT, k=2, h=GH)
        U = region(1024).rearrange("p (t h n) -> p t h n", t=NT, h=GH)
        wT = region(1024).rearrange("p (t h n) -> p t h n", t=NT, h=GH)
        VN = region(1024).rearrange("p (t h n) -> p t h n", t=NT, h=GH)
        S = region(512).rearrange("p (h n) -> p h n", h=GH)
        on = region(1024).rearrange("p (t h n) -> p t h n", t=NT, h=GH)
        gdn_top = top[0]
        square = pool[:, ring_floats + 1040:ring_floats + 1040 + 2048].rearrange("p (j t) -> p j t", j=8)
        diag = pool[:, ring_floats + 1040 + 2048:ring_floats + 1040 + 4096].rearrange("p (t k h n) -> p t k h n", t=NT, k=2, h=GH)
        top[0] = shared
        hl = region(RW_TILES * T).rearrange("p (j t) -> p j t", j=RW_TILES)
        lw = region(1024).rearrange("p (t n) -> p t n", t=NT)
        aT = region(1024).rearrange("p (j t) -> p j t", j=RP)
        bonus = region(1024).rearrange("p (j t) -> p j t", j=RP)
        kkT = region(1024).rearrange("p (j t) -> p j t", j=RP)
        TK = region(2048).rearrange("p (t k n) -> p t k n", t=NT, k=4)
        E = pool[:, shared + RW_TILES * T + 4096:shared + RW_TILES * T + 4096 + 1536].rearrange(
            "p (t j k n) -> p t j k n", t=NT, j=2, k=3)
        G4 = region(4096).rearrange("p (i k n) -> p i k n", i=8, k=4)
        g4_at = shared + RW_TILES * T + 4096 + 2048
        rsq = pool[:, g4_at:g4_at + 1024].rearrange("p (j t) -> p j t", j=RP)
        rtmp = pool[:, g4_at + 1024:g4_at + 2048].rearrange("p (j t) -> p j t", j=RP)
        ysq = pool[:, g4_at:g4_at + 1024].rearrange("p (t n) -> p t n", t=NT)
        rtmp2 = pool[:, g4_at + 2048:g4_at + 3072].rearrange("p (j t) -> p j t", j=RP)
        Av = region(512).rearrange("p (t j n) -> p t j n", t=NT, j=2)
        RU = region(512).rearrange("p (t j n) -> p t j n", t=NT, j=2)
        RC = region(512).rearrange("p (t j n) -> p t j n", t=NT, j=2)
        WcT = region(512).rearrange("p (t j n) -> p t j n", t=NT, j=2)
        Z = region(NCH * 256).rearrange("p (c j n) -> p c j n", c=NCH, j=2)
        Ec = region(16).rearrange("p (t j n) -> p t j n", t=NT, j=2)
        Dc = region(8).rearrange("p (j n) -> p j n", j=2)
        rw_top = top[0]
        KR = hn[:, 0, :].rearrange("p (t j k n) -> p t j k n", t=NT, j=2, k=2)
        BK = hn[:, 1, :].rearrange("p (t j k n) -> p t j k n", t=NT, j=2, k=2)
        y_tok = oT[:, 2].rearrange("p h t -> p (h t)").rearrange("p (t n) -> p t n", t=NT)
        top[0] = shared
        qkT = region(8 * T).rearrange("p (j t) -> p j t", j=8)
        sv = region(1024).rearrange("p (t n) -> p t n", t=NT)
        absz = region(768).rearrange("p (b n) -> p b n", b=2)
        sp = region(768).rearrange("p (b n) -> p b n", b=2)
        att = region(768).rearrange("p (b n) -> p b n", b=2)
        mT = region(KD * T).rearrange("p (j t) -> p j t", j=KD)
        gate = region(1024).rearrange("p (b n) -> p b n", b=2)
        mtmp = region(512)
        top[0] = MRING * SLOT
        ffT = region(22 * T).rearrange("p (j t) -> p j t", j=22)
        sg = region(512).rearrange("p (b n) -> p b n", b=2)
        top[0] = MRING * SLOT
        xgT = region(KD * CAP).rearrange("p (k n) -> p k n", k=KD)
        heT = region(FT * CAP).rearrange("p (j n) -> p j n", j=FT)
        sge = region(2 * CAP).rearrange("p (b n) -> p b n", b=2)
        sel = region(NT * CAP).rearrange("p (t n) -> p t n", t=NT)
        selw = region(NT * CAP).rearrange("p (t n) -> p t n", t=NT)
        selwT = region(T)
        ye = hnT[:, 0:4, :].rearrange("p k t -> p (k t)")
        fgain = hnT[:, 4:8, :].rearrange("p k t -> p (k t)")
        rt = region(NT * 16 * NE).rearrange("p (t k e) -> p t k e", t=NT, k=16)
        rs = region(64)
        table = region(32)
        selb = region(NT * CAP).rearrange("p (t n) -> p t n", t=NT)
        pass_expert = sb("pass_expert", [1, 32], I32)

        vec_loaded = sem("vec_loaded")
        par_loaded = sem("par_loaded")
        x_loaded = sem("x_loaded")
        fgain_loaded = sem("fgain_loaded")
        consts_ready = sem("consts_ready")
        pool_step = sem("pool_step")
        vec_mm = sem("vec_mm")
        vec_ready = sem("vec_ready")
        slot_loaded = [sem(f"slot{i}_loaded") for i in range(MRING)]
        out_stored = sem("out_stored")
        dve_step = sem("dve_step")
        act_step = sem("act_step")

        loads = []
        slot_count = [0] * MRING
        slot_last = [None] * MRING
        turn = [0]

        def add_load(src, view, ring=RING):
            s = turn[0] % ring
            turn[0] = s + 1
            slot_count[s] += 1
            loads.append((src, view, s, slot_count[s], slot_last[s]))
            slot_last[s] = len(loads) - 1
            return len(loads) - 1

        tiled = lambda w: w.rearrange("(k p) n -> p k n", p=P)
        L = []
        for l in range(DEPTH):
            it = {}

            def cols(lo, n, w=tiled(a["w_in"][l])):
                return add_load(w[:, :, lo:lo + n], (KD, n))

            it["qkv"] = [cols(SW * i, SW) for i in range(6)]
            it["ba"] = cols(O_BA, 8)
            it["z"] = [cols(O_Z + SW * i, SW) for i in range(2)]
            it["rw"] = [cols(O_RW + SW * i, SW) for i in range(7)]
            it["sb"] = [cols(O_SB + SW * i, SW) for i in range(6)]
            it["merge"] = []
            for b, name in enumerate(("w_branch_gdn", "w_branch_rwkv", "w_branch_sb")):
                for i in range(2):
                    lo = O_GATE + b * D + 512 * i
                    it["merge"].append((cols(lo, SW), add_load(tiled(a[name][l])[:, :, 512 * i:512 * i + 512], (4, 512)),
                                        cols(lo + SW, SW)))
            it["out"] = [add_load(tiled(a["w_out"][l])[:, :, SW * i:SW * i + SW], (KD, SW)) for i in range(4)]
            if l == 0:
                it["ffn_first"] = len(loads)
                it["ffn"] = []
                for f in range(0, FFD, SW):
                    it["ffn"].append((
                        add_load(tiled(a["ffn_w_gate"][0])[:, :, f:f + SW], (KD, SW), MRING),
                        add_load(tiled(a["ffn_w_up"][0])[:, :, f:f + SW], (KD, SW), MRING),
                        add_load(tiled(a["ffn_w_down"][0][f:f + SW, :]), (SW // P, D), MRING)))
            L.append(it)
        n_loads = len(loads)

        def weights(n):
            k, m = loads[n][1]
            return slot(loads[n][2])[:, 0:k * m].rearrange("p (k n) -> p k n", k=k)

        xnorm_ready = sig("xnorm_ready", 4)
        hnT_mm = sig("hnT_mm", 8)
        hnT_ready = sig("hnT_ready", 8)
        proj_mm = sig("proj_mm", 45)
        raw_ready = sig("raw_ready", 13)
        raw_used = sig("raw_used", 13)
        zt_ready = sig("zt_ready", 2)
        ba_mm = sig("ba_mm", 1)
        ba_abs = sig("ba_abs", 1)
        ba_ln = sig("ba_ln", 1)
        lnr_ready = sig("lnr_ready", 1)
        expo_scal = sig("expo_scal", 1)
        osq_ready = sig("osq_ready", 2)
        oss_ready = sig("oss_ready", 2)
        ors_ready = sig("ors_ready", 2)
        rms_ready = sig("rms_ready", 2)
        ysum_ready = sig("ysum_ready", 1)
        ysq_ready = sig("ysq_ready", 1)
        yvar_ready = sig("yvar_ready", 1)
        yrs_ready = sig("yrs_ready", 1)
        g_ready = sig("g_ready", 1)
        qkv_silu = sig("qkv_silu", 3)
        square_ready = sig("square_ready", 1)
        stats_mm = sig("stats_mm", 1)
        scal_ready = sig("scal_ready", 1)
        diag_ready = sig("diag_ready", 4)
        bcast_mm = sig("bcast_mm", 4)
        qfac_ready = sig("qfac_ready", 2)
        kv_mm = sig("kv_mm", 4)
        kv_read = sig("kv_read", 4)
        qdec_ready = sig("qdec_ready", 2)
        expo_ready = sig("expo_ready", 4)
        decay_ready = sig("decay_ready", 4)
        gram_mm = sig("gram_mm", 4)
        gram_read = sig("gram_read", 4)
        ml_ready = sig("ml_ready", 6 * 6)
        xt0_ready = sig("xt0_ready", 6)
        x0_mm = sig("x0_mm", 6)
        x0_ready = sig("x0_ready", 6)
        y_mm = sig("y_mm", 30)
        y_ready = sig("y_ready", 30)
        x_mm = sig("x_mm", 30)
        x_ready = sig("x_ready", 30)
        uw_mm = sig("uw_mm", 4)
        uw_ready = sig("uw_ready", 4)
        s_ready = sig("s_ready", 4)
        vn_mm = sig("vn_mm", 4)
        vn_ready = sig("vn_ready", 4)
        s_mm = sig("s_mm", 3)
        o_mm = sig("o_mm", 2)
        on_ready = sig("on_ready", 2)
        onT_mm = sig("onT_mm", 2)
        oa_ready = sig("oa_ready", 2)
        lora_in = sig("lora_in", 2)
        u_mm = sig("u_mm", 2)
        a_mm = sig("a_mm", 2)
        u_ready = sig("u_ready", 2)
        lw_ready = sig("lw_ready", 1)
        a_ready = sig("a_ready", 1)
        kk2_ready = sig("kk2_ready", 1)
        kk2_mm = sig("kk2_mm", 2)
        rk_ready = sig("rk_ready", 1)
        rk_mm = sig("rk_mm", 2)
        krs_ready = sig("krs_ready", 1)
        feat_ready = sig("feat_ready", 1)
        L_mm = sig("L_mm", 8)
        E_ready = sig("E_ready", 8)
        krbk_ready = sig("krbk_ready", 8)
        tk_mm = sig("tk_mm", 8)
        tk_ready = sig("tk_ready", 8)
        g4_mm = sig("g4_mm", 16)
        g4_ready = sig("g4_ready", 16)
        av_mm = sig("av_mm", 2)
        av_ready = sig("av_ready", 2)
        rw_mm = sig("rw_mm", 4)
        rw_ready = sig("rw_ready", 4)
        z_ready = sig("z_ready", 8)
        c_mm = sig("c_mm", 8)
        c_ready = sig("c_ready", 8)
        z_mm = sig("z_mm", 6)
        ry_mm = sig("ry_mm", 4)
        ry_ready = sig("ry_ready", 4)
        yn_ready = sig("yn_ready", 1)
        ynT_mm = sig("ynT_mm", 2)
        rgate_mm = sig("rgate_mm", 2)
        ob_ready = sig("ob_ready", 2)
        z_scores = sig("z_scores", 8)
        l1_ready = sig("l1_ready", 8)
        sp_raw = sig("sp_raw", 8)
        sp_ready = sig("sp_ready", 8)
        loga_mm = sig("loga_mm", 8)
        att_raw = sig("att_raw", 8)
        att_ready = sig("att_ready", 8)
        pv_mm = sig("pv_mm", 8)
        qk_ready = sig("qk_ready", 4)
        oc_ready = sig("oc_ready", 4)
        sv_ready = sig("sv_ready", 2)
        gate_ready = sig("gate_ready", 12)
        merge_step = sig("merge_step", 12)
        xo_mm = sig("xo_mm", 4)
        xo_ready = sig("xo_ready", 4)
        ff_mm = sig("ff_mm", 22)
        ff_silu = sig("ff_silu", 22)
        ff_ready = sig("ff_ready", 22)
        down_mm = sig("down_mm", 11)
        fx_ready = sig("fx_ready", 1)
        once = [ff_mm, ff_silu, ff_ready, down_mm, fx_ready]
        logit_mm = sem("logit_mm")
        oneh_ready = sem("oneh_ready")
        rank_mm = sem("rank_mm")
        passes_ready = sem("passes_ready")
        sel_ready = sem("sel_ready")
        gather_mm = sem("gather_mm")
        xg_ready = sem("xg_ready")
        selT_mm = sem("selT_mm")
        selT_ready = sem("selT_ready")
        he_silu = sem("he_silu")
        he_ready = sem("he_ready")
        ye_ready = sem("ye_ready")
        sc_mm = sem("sc_mm")
        sc_added = sem("sc_added")
        fin_ready = sem("fin_ready")
        frms_ready = sem("frms_ready")
        margin_ready = sem("margin_ready")
        seld = sem("sel_parts_ready")
        all_added = sem("all_added")
        marg_exp = sem("marg_exp")

        def over(ap, n):
            return ap.unsqueeze(2).to_broadcast([ap.shape[0], ap.shape[1], n])

        def rep(ap, n):
            return ap.unsqueeze(1).to_broadcast([ap.shape[0], n, ap.shape[1]])

        freed = {}
        hid_base = DEPTH * proj_mm.per_layer
        down_base = down_mm.per_layer

        block = ctx.enter_context(nc.Block())

        @block.gpsimd
        def _(gp):
            steps = [0]

            def link(ins):
                steps[0] += 1
                ins.then_inc(pool_step, 1)
                gp.wait_ge(pool_step, steps[0])

            def keep(dst, src, pattern, base, mult, op, fill=0.0):
                link(gp.affine_select(out=dst, in_=src, pattern=pattern, compare_op=op, fill=fill, base=base,
                                      channel_multiplier=mult))

            link(gp.memset(ones[:], 1.0))
            link(gp.memset(neg_ones[:], -1.0))
            keep(ident[:], ones[:], [[-1, P]], 0, 1, ALU.is_equal)

            def block_of(dst, src, n):
                d3 = dst.rearrange("p (b i) -> p b i", i=n)
                s3 = src.rearrange("p (b i) -> p b i", i=n)
                keep(d3, s3, [[-n, P // n], [0, n]], 0, 1, ALU.is_ge)
                keep(d3, d3, [[n, P // n], [0, n]], n - 1, -1, ALU.is_ge)

            block_of(same_chunk[:], ones[:], C)
            keep(incl[:], same_chunk[:], [[1, P]], 0, -1, ALU.is_ge)
            keep(strict[:], same_chunk[:], [[1, P]], -1, -1, ALU.is_ge)
            keep(before[:], ones[:], [[1, P]], -1, -1, ALU.is_ge)
            link(gp.tensor_scalar(neg_incl[:], incl[:], -NEG, NEG, ALU.mult, ALU.add))
            link(gp.tensor_scalar(neg_strict[:], strict[:], -NEG, NEG, ALU.mult, ALU.add))
            link(gp.tensor_copy(gram_mask[:, 0, :], strict[:]))
            link(gp.tensor_scalar(gram_mask[:, 1, :], incl[:], -1.0, None, ALU.mult))
            link(gp.tensor_copy(gram_mask[:, 2, :], strict[:]))
            link(gp.tensor_copy(gram_mask[:, 3, :], incl[:]))
            for b in range(6):
                n = 1 << b
                block_of(level_mask[:, b, :], ones[:], 2 * n)
                m4 = level_mask[:, b, :].rearrange("p (b i) -> p b i", i=2 * n)
                keep(m4, m4, [[0, P // (2 * n)], [1, 2 * n]], -n, 0, ALU.is_ge)
                keep(m4, m4, [[2 * n, P // (2 * n)], [0, 2 * n]], n - 1, -1, ALU.is_ge)
            half = tri_mid[:, 0:P]
            h3 = half.rearrange("p (b i) -> p b i", i=C)
            keep(h3, same_chunk[:].rearrange("p (b i) -> p b i", i=C), [[C, P // C], [0, C]], C // 2 - 1, -1, ALU.is_ge)
            for c in range(2):
                link(gp.tensor_scalar(tri_mid[:, 2 * P + 2 + c:2 * P + 3 + c], tri_mid[:, C * c:C * c + 1], -W_FACTOR,
                                      None, ALU.mult))
                link(gp.tensor_tensor(tri_mid[:, 2 * P + c:2 * P + 1 + c], same_chunk[:, C * c:C * c + 1],
                                      tri_mid[:, C * c:C * c + 1], ALU.subtract))
                link(gp.tensor_scalar(tri_mid[:, 2 * P + c:2 * P + 1 + c], tri_mid[:, 2 * P + c:2 * P + 1 + c],
                                      -W_FACTOR, None, ALU.mult))
            link(gp.tensor_tensor(tri_mid[:, P:2 * P], strict[:], half, ALU.subtract))
            link(gp.tensor_tensor(half, incl[:], half, ALU.subtract))
            link(gp.tensor_scalar(tri_mid[:, 0:2 * P], tri_mid[:, 0:2 * P], -W_FACTOR, None, ALU.mult))
            keep(neg_suffix[:], neg_ones[:], [[-1, P]], 0, 1, ALU.is_ge)
            for c in range(2):
                keep(chunk_rows[:, c, :], ones[:], [[0, P]], -C * c, 1, ALU.is_ge)
                keep(chunk_rows[:, c, :], chunk_rows[:, c, :], [[0, P]], C * c + C - 1, -1, ALU.is_ge)
            link(gp.iota(slots_iota[:], pattern=[[1, CAP]], base=0, channel_multiplier=0,
                         allow_small_or_imprecise_dtypes=True))
            for i, v in enumerate((RMS_EPS, L2_EPS, GN_EPS)):
                link(gp.memset(eps_c[:, i:i + 1], v))
            gp.memset(eps_c[:, 3:4], 1.0).then_inc(consts_ready, 1)

            def solver_levels(l, run, m_ready, m_count, m_of):
                for b in range(6):
                    for g in range(2):
                        if b == 0:
                            m_ready.wait(gp, l, m_count[g])
                        elif b == 1:
                            xt0_ready.wait(gp, l, 2 * run + g + 1)
                        else:
                            y_mm.wait(gp, l, 10 * run + 2 * (b - 2) + g + 1)
                        ml_ready.by(gp.tensor_tensor(Ml[:, 4 * g:4 * g + 4, :], m_of(g),
                                                     rep(level_mask[:, b, :], 4), ALU.mult))

            for l in range(DEPTH):
                solver_levels(l, 0, gram_read, (4, 4), lambda g: EE[:, g, 0, :, :])
                for q in range(2):
                    solver_levels(l, 1 + q, g4_ready, (8 * q + 4, 8 * q + 8), lambda g: G4[:, 4 * g:4 * g + 4, 0, :])
                for h in range(8):
                    b2 = lambda t: t[:, h % 2, :].rearrange("p (b n) -> p b n", b=3)[:, 0:3:2, :]
                    pat = [[0, 2], [1, P]]
                    sp_raw.wait(gp, l, h + 1)
                    sp_ready.by(gp.affine_select(out=b2(sp), in_=b2(sp), pattern=pat, compare_op=ALU.is_ge, fill=0.0,
                                                 base=-1, channel_multiplier=-1))
                    att_raw.wait(gp, l, h + 1)
                    att_ready.by(gp.affine_select(out=b2(att), in_=b2(att), pattern=pat, compare_op=ALU.is_ge, fill=0.0,
                                                  base=-1, channel_multiplier=-1))

        @block.tensor
        def _(pe):
            mm = pe.matmul

            def arrived(n):
                pe.wait_ge(slot_loaded[loads[n][2]], 16 * loads[n][3])

            def release(n, signal):
                freed[n] = (signal.handle, signal.given)

            readers = []

            def proj_bank(l, reader, count):
                n = len(readers)
                readers.append((reader, l, count))
                if n >= 2:
                    signal, ll, c = readers[n - 2]
                    signal.wait(pe, ll, c)
                return proj[n % 2]

            def proj_tiles(l, n, reader, count):
                arrived(n)
                w = weights(n)
                tiles = loads[n][1][1] // P
                for j in range(0, tiles, 2):
                    ps = proj_bank(l, reader, count + j // 2 + 1)
                    for s in range(2):
                        for k in range(KD):
                            ins = mm(ps[:, s * T:(s + 1) * T], w[:, k, (j + s) * P:(j + s + 1) * P], hnT[:, k, :],
                                     start=(k == 0), stop=(k == KD - 1))
                    proj_mm.by(ins)
                release(n, proj_mm)

            def transposes_of_hn(l, half):
                for t in range(NT):
                    xnorm_ready.wait(pe, l, 2 * half + t + 1)
                    for q in range(2):
                        i = 4 * half + 2 * t + q
                        for k in range(4):
                            ins = pe.transpose(B[2 * t + q][:, k * P:(k + 1) * P],
                                               hn[:, t, (4 * q + k) * P:(4 * q + k + 1) * P], ident[:])
                        hnT_mm.by(ins)

            def solver(l, run):
                for g in range(2):
                    xt0_ready.wait(pe, l, 2 * run + g + 1)
                    for i in range(4):
                        ins = pe.transpose(B[2 + g][:, i * P:(i + 1) * P], XT[:, 4 * g + i, :], ident[:])
                    x0_mm.by(ins)
                for b in range(1, 6):
                    for g in range(2):
                        n = 10 * run + 2 * (b - 1) + g
                        ml_ready.wait(pe, l, 12 * run + 2 * b + g + 1)
                        if b == 1:
                            x0_ready.wait(pe, l, 2 * run + g + 1)
                        else:
                            x_ready.wait(pe, l, n - 2 + 1)
                        for i in range(4):
                            ins = mm(B[g][:, i * P:(i + 1) * P], Ml[:, 4 * g + i, :], X[:, 4 * g + i, :],
                                     start=True, stop=True)
                        y_mm.by(ins)
                    for g in range(2):
                        n = 10 * run + 2 * (b - 1) + g
                        y_ready.wait(pe, l, n + 1)
                        for i in range(4):
                            if b < 5:
                                mm(B[2 + g][:, i * P:(i + 1) * P], XT[:, 4 * g + i, :], Y[:, 4 * g + i, :],
                                   start=True, stop=True)
                            ins = mm(B[4 + g][:, i * P:(i + 1) * P], Y[:, 4 * g + i, :], XT[:, 4 * g + i, :],
                                     start=True, stop=True)
                        x_mm.by(ins)

            def deltanet(l):
                for i, n in enumerate(L[l]["qkv"]):
                    proj_tiles(l, n, raw_ready, i)
                n = L[l]["ba"]
                arrived(n)
                for t in range(NT):
                    for k in range(KD):
                        ins = mm(B[4][:, 8 * t:8 * t + 8], hnT[:, k, t * P:(t + 1) * P], weights(n)[:, k, :],
                                 start=(k == 0), stop=(k == KD - 1))
                ba_mm.by(ins)
                release(n, ba_mm)
                for i, n in enumerate(L[l]["z"]):
                    proj_tiles(l, n, zt_ready, i)
                square_ready.wait(pe, l, 1)
                for t in range(NT):
                    for j in range(8):
                        mm(B[5][:, 16 + 8 * t + j:17 + 8 * t + j], square[:, j, t * P:(t + 1) * P], ones[:, 0:1],
                           start=True, stop=True)
                g_ready.wait(pe, l, 1)
                g = stat[:, 0:8]
                for t in range(NT):
                    gt = g[:, 4 * t:4 * t + 4]
                    mm(B[5][:, 32 + 4 * t:36 + 4 * t], incl[:], gt, start=True, stop=True)
                    mm(B[5][:, 40 + 4 * t:44 + 4 * t], same_chunk[:], gt, start=True, stop=True)
                    for c in range(2):
                        ins = mm(B[5][:, 48 + 8 * t + 4 * c:52 + 8 * t + 4 * c], chunk_rows[:, c, :], gt,
                                 start=True, stop=True)
                stats_mm.by(ins)
                qkv_silu.wait(pe, l, 3)
                for kind in range(2):
                    for t in range(NT):
                        for h in range(GH):
                            ins = pe.transpose(B[2 * kind + t][:, h * P:(h + 1) * P],
                                               qkv[:, 4 + 4 * kind + h, t * P:(t + 1) * P], ident[:])
                        kv_mm.by(ins)
                for t in range(NT):
                    for k in range(2):
                        n = 2 * t + k
                        diag_ready.wait(pe, l, n + 1)
                        if n >= 2:
                            expo_ready.wait(pe, l, n - 1)
                            if k == 1:
                                qfac_ready.wait(pe, l, 1)
                        bcast_mm.by(mm(B[4 + k][:, :], ones[:], diag[:, t, k, :, :], start=True, stop=True))
                for t in range(NT):
                    for k in range(2):
                        n = 2 * t + k
                        kv_read.wait(pe, l, 4)
                        for h in range(GH):
                            rhs = qkv[:, (4 if k == 0 else 0) + h, t * P:(t + 1) * P]
                            ins = mm(B[2 * t + k][:, h * P:(h + 1) * P], qkv[:, 4 + h, t * P:(t + 1) * P], rhs,
                                     start=True, stop=True)
                        gram_mm.by(ins)
                gram_read.wait(pe, l, 4)
                expo_ready.wait(pe, l, 4)
                qfac_ready.wait(pe, l, 2)
                solver(l, 0)
                for g in range(2):
                    x_ready.wait(pe, l, 8 + g + 1)
                for t in range(NT):
                    for h in range(GH):
                        ins = mm(B[t][:, h * P:(h + 1) * P], XT[:, 4 * t + h, :], vb[:, t, h, :], start=True, stop=True)
                    uw_mm.by(ins)
                for t in range(NT):
                    for h in range(GH):
                        ins = mm(B[2 + t][:, h * P:(h + 1) * P], kb[:, t, h, :], XT[:, 4 * t + h, :], start=True, stop=True)
                    uw_mm.by(ins)
                uw_ready.wait(pe, l, 4)
                for c in range(NCH):
                    t, b = c // 2, C * (c % 2)
                    rows = slice(b, b + C)
                    s_ready.wait(pe, l, c + 1)
                    for h in range(GH):
                        ins = mm(B[4][rows, h * P:(h + 1) * P], wT[:, t, h, rows], S[:, h, :], start=True, stop=True)
                    vn_mm.by(ins)
                    for h in range(GH):
                        mm(B[t][rows, h * P:(h + 1) * P], qdec[:, t, h, rows], S[:, h, :], start=(h == 0), stop=False,
                           skip_group_check=True)
                    vn_ready.wait(pe, l, c + 1)
                    for h in range(GH if c < NCH - 1 else 0):
                        ins = mm(B[5][:, h * P:(h + 1) * P], kdec[rows, t, h, :], VN[rows, t, h, :], start=True, stop=True)
                    if c < NCH - 1:
                        s_mm.by(ins)
                    if c % 2:
                        for h in range(GH):
                            ins = mm(B[t][:, h * P:(h + 1) * P], EE[:, t, 1, h, :], VN[:, t, h, :], start=False,
                                     stop=(h == GH - 1), skip_group_check=True)
                        o_mm.by(ins)
                for t in range(NT):
                    on_ready.wait(pe, l, t + 1)
                    for h in range(GH):
                        ins = pe.transpose(B[2 + t][:, h * P:(h + 1) * P], on[:, t, h, :], ident[:])
                    onT_mm.by(ins)

            def rwkv(l):
                for i, n in enumerate(L[l]["rw"]):
                    proj_tiles(l, n, raw_ready, 6 + i)
                lora_in.wait(pe, l, 1)
                oa_ready.wait(pe, l, 2)
                for t in range(NT):
                    u_mm.by(mm(B[t][:, :], hl[0:64, 12, t * P:(t + 1) * P], lora[0:64, l, :], start=True, stop=True))
                for q in range(2):
                    for s in range(2):
                        j = 2 * q + s
                        ins = mm(B[2 + q][:, s * T:(s + 1) * T], lora[64:128, l, j * P:(j + 1) * P], hl[64:128, 12, :],
                                 start=True, stop=True)
                    a_mm.by(ins)
                kk2_ready.wait(pe, l, 1)
                for q in range(2):
                    kk2_mm.by(mm(B[4 + q][:, :], same_chunk[:], rsq[:, 2 * q:2 * q + 2, :], start=True, stop=True))
                rk_ready.wait(pe, l, 1)
                u_ready.wait(pe, l, 2)
                for q in range(2):
                    rk_mm.by(mm(B[q][:, :], same_chunk[:], rtmp[:, 2 * q:2 * q + 2, :], start=True, stop=True))
                lw_ready.wait(pe, l, 1)
                feat_ready.wait(pe, l, 1)
                for q in range(2):
                    a_ready.wait(pe, l, 1)
                    ry_ready.wait(pe, l, 2 * q)
                    for t in range(NT):
                        for j in range(2):
                            p = 2 * q + j
                            L_mm.by(mm(B[2 * t + j][:, 0:2 * P + 4], lw[:, t, p * P:(p + 1) * P], tri_mid[:],
                                       start=True, stop=True))
                    for t in range(NT):
                        for k in range(2):
                            bank = (B[4], B[5], B[0], B[1])[2 * t + k]
                            krbk_ready.wait(pe, l, 4 * q + 2 * t + 2)
                            if t:
                                E_ready.wait(pe, l, 4 * q + 4)
                            srcs = ((lambda j: KR[:, t, j, 0, :]), (lambda j: BK[:, t, j, 0, :])) if k == 0 else (
                                (lambda j: BK[:, t, j, 1, :]), (lambda j: hl[:, 8 + 2 * q + j, t * P:(t + 1) * P]))
                            for s in range(2):
                                for j in range(2):
                                    ins = pe.transpose(bank[:, (2 * s + j) * P:(2 * s + j + 1) * P], srcs[s](j), ident[:])
                            tk_mm.by(ins)
                    E_ready.wait(pe, l, 4 * q + 4)
                    for t in range(NT):
                        for j in range(2):
                            for e in range(2):
                                i = 4 * t + 2 * j + e
                                n = 8 * q + i
                                rows = slice(64 * e, 64 * e + 64)
                                if i >= 2:
                                    g4_ready.wait(pe, l, n - 1)
                                bank = B[2 + i % 2]
                                for s in range(2):
                                    ins = mm(bank[:, s * T:(s + 1) * T], BK[rows, t, j, s, :],
                                             KR[rows, t, j, :, :], start=True, stop=True)
                                g4_mm.by(ins)
                    g4_ready.wait(pe, l, 8 * q + 8)
                    tk_ready.wait(pe, l, 4 * q + 4)
                    solver(l, 1 + q)
                    for i in range(8):
                        t, j, e = i // 4, i // 2 % 2, i % 2
                        if i == 0:
                            x_ready.wait(pe, l, 10 * (1 + q) + 10)
                        ins = mm(B[0][:, i * 64:(i + 1) * 64], G4[:, i, 2, :],
                                 TK[:, t, 3, j * P + 64 * e:j * P + 64 * e + 64], start=True, stop=True)
                    av_mm.by(ins)
                    for i in range(8):
                        t, j, e = i // 4, i // 2 % 2, i % 2
                        ins = mm(B[2][64 * e:64 * e + 64, (2 * t + j) * P:(2 * t + j + 1) * P],
                                 TK[:, t, 0, j * P + 64 * e:j * P + 64 * e + 64], XT[:, i, :], start=True, stop=True)
                    rw_mm.by(ins)
                    av_ready.wait(pe, l, q + 1)
                    for i in range(8):
                        t, j, e = i // 4, i // 2 % 2, i % 2
                        ins = mm(B[1][:, i * 64:(i + 1) * 64], XT[:, i, :], Av[:, t, j, 64 * e:64 * e + 64],
                                 start=True, stop=True)
                    rw_mm.by(ins)
                    rw_ready.wait(pe, l, 2 * q + 2)
                    for c in range(NCH):
                        t, b = c // 2, C * (c % 2)
                        rows = slice(b, b + C)
                        n = 4 * q + c
                        ybank = (B[5], B[0])[t]
                        z_ready.wait(pe, l, n + 1)
                        for j in range(2):
                            ins = mm(B[3][rows, j * P:(j + 1) * P], WcT[:, t, j, rows], Z[:, c, j, :], start=True, stop=True)
                        c_mm.by(ins)
                        for j in range(2):
                            mm(ybank[rows, j * P:(j + 1) * P], KR[:, t, j, 1, rows], Z[:, c, j, :], start=(j == 0),
                               stop=False, skip_group_check=True)
                        c_ready.wait(pe, l, n + 1)
                        for j in range(2 if c < NCH - 1 else 0):
                            cs = slice(j * P, (j + 1) * P)
                            mm(B[4][:, cs], TK[rows, t, 2, cs], TK[rows, t, 3, cs], start=True, stop=False)
                            ins = mm(B[4][:, cs], TK[rows, t, 1, cs], RC[rows, t, j, :], start=False, stop=True)
                        if c < NCH - 1:
                            z_mm.by(ins)
                        if c % 2:
                            for j in range(2):
                                for e in range(2):
                                    i = 4 * t + 2 * j + e
                                    cs = slice(j * P + 64 * e, j * P + 64 * e + 64)
                                    mm(ybank[:, cs], G4[:, i, 3, :], TK[:, t, 3, cs], start=False, stop=False,
                                       skip_group_check=True)
                                    ins = mm(ybank[:, cs], G4[:, i, 1, :], RC[:, t, j, 64 * e:64 * e + 64], start=False,
                                             stop=(j == 1 and e == 1), skip_group_check=True)
                            ry_mm.by(ins)
                for q in range(2):
                    ry_ready.wait(pe, l, 4)
                    lora_in.wait(pe, l, 2)
                    for s in range(2):
                        j = 2 * q + s
                        ins = mm(B[3 + q][:, s * T:(s + 1) * T], g2[:, l, j * P:(j + 1) * P], hl[:, 13, :],
                                 start=True, stop=True)
                    rgate_mm.by(ins)
                yn_ready.wait(pe, l, 1)
                for t in range(NT):
                    for j in range(RP):
                        ins = pe.transpose(B[1 + t][:, j * P:(j + 1) * P], y_tok[:, t, j * P:(j + 1) * P], ident[:])
                    ynT_mm.by(ins)

            def attention(l):
                for i, n in enumerate(L[l]["sb"][:4]):
                    proj_tiles(l, n, qk_ready, i)
                for t in range(NT):
                    ps = proj_bank(l, sv_ready, t + 1)
                    for half, n in enumerate(L[l]["sb"][4:]):
                        arrived(n)
                        for k in range(KD):
                            ins = mm(ps[:, half * SW:(half + 1) * SW], hnT[:, k, t * P:(t + 1) * P], weights(n)[:, k, :],
                                     start=(k == 0), stop=(k == KD - 1))
                    proj_mm.by(ins)
                for n in L[l]["sb"][4:]:
                    release(n, proj_mm)
                ob_ready.wait(pe, l, 2)
                qk_ready.wait(pe, l, 4)
                sv_ready.wait(pe, l, 2)

                def scores(h):
                    j, e = h // 2, h % 2
                    rows = slice(64 * e, 64 * e + 64)
                    bank = B[h % 4]
                    if h >= 4:
                        att_raw.wait(pe, l, h - 3)
                    mm(bank[:, 0:T], qkT[rows, 4 + j, 0:P], qkT[rows, j, :], start=True, stop=False,
                       skip_group_check=True)
                    z_scores.by(mm(bank[:, T:T + P], qkT[rows, 4 + j, P:T], qkT[rows, j, P:T], start=False, stop=False,
                                   skip_group_check=True))

                def sums(h):
                    bank = B[h % 4]
                    sp_ready.wait(pe, l, h + 1)
                    mm(bank[:, 0:384], neg_suffix[:], sp[:, h % 2, :], start=False, stop=False, skip_group_check=True)
                    loga_mm.by(mm(bank[:, P:T], neg_ones[:], sp[:, h % 2, T:T + P], start=False, stop=True,
                                  skip_group_check=True))

                def values(h):
                    j, e = h // 2, h % 2
                    bank = B[4 + j % 2]
                    if e == 0 and j >= 2:
                        oc_ready.wait(pe, l, j - 1)
                    att_ready.wait(pe, l, h + 1)
                    rows = slice(64 * e, 64 * e + 64)
                    cs = slice(64 * h, 64 * h + 64)
                    mm(bank[rows, 0:T], sv[:, 0, cs], att[:, h % 2, 0:T], start=True, stop=False, skip_group_check=True)
                    ins = mm(bank[rows, P:T], sv[:, 1, cs], att[:, h % 2, T:T + P], start=False, stop=True,
                             skip_group_check=True)
                    pv_mm.by(ins)

                scores(0)
                for h in range(8):
                    if h < 7:
                        scores(h + 1)
                    sums(h)
                    values(h)

            def merge(l):
                for i, (g0, nb, g1) in enumerate(L[l]["merge"]):
                    for jp, ng in enumerate((g0, g1)):
                        m = 2 * i + jp + 1
                        for n, j0, src, kt, reader in ((ng, 0, hnT, KD, gate_ready),
                                                       (nb, 2 * jp, oT[:, i // 2], GH, merge_step)):
                            arrived(n)
                            ps = proj_bank(l, reader, m)
                            for s in range(2):
                                for k in range(kt):
                                    ins = mm(ps[:, s * T:(s + 1) * T], weights(n)[:, k, (j0 + s) * P:(j0 + s + 1) * P],
                                             src[:, k, :], start=(k == 0), stop=(k == kt - 1))
                            proj_mm.by(ins)
                            if n == ng or jp == 1:
                                release(n, proj_mm)
                for half in range(2):
                    for t in range(NT):
                        if half == 0 and t == 0:
                            merge_step.wait(pe, l, 12)
                            oc_ready.wait(pe, l, 4)
                        bank = B[2 * half + t]
                        for s in range(2):
                            n = L[l]["out"][2 * half + s]
                            arrived(n)
                            for k in range(KD):
                                ins = mm(bank[:, s * SW:(s + 1) * SW], mT[:, k, t * P:(t + 1) * P], weights(n)[:, k, :],
                                         start=(k == 0), stop=(k == KD - 1))
                        xo_mm.by(ins)
                    for s in range(2):
                        release(L[l]["out"][2 * half + s], xo_mm)

            def dense_ffn(l):

                def down_tile(f, n, i):
                    ff_ready.wait(pe, 0, f + 1)
                    arrived(n)
                    for t in range(NT):
                        for half in range(2):
                            ins = mm(B[2 * t + half][:, :], ffT[:, f, t * P:(t + 1) * P],
                                     weights(n)[:, i, half * 512:half * 512 + 512], start=(f == 0),
                                     stop=(f == FFD // P - 1))
                    if i == loads[n][1][0] - 1:
                        down_mm.by(ins)
                        release(n, down_mm)

                former = None
                for c, (g, u, d) in enumerate(L[l]["ffn"]):
                    arrived(g)
                    arrived(u)
                    tiles = loads[g][1][1] // P
                    for i in range(tiles):
                        f = 2 * c + i
                        if f >= 2:
                            ff_ready.wait(pe, 0, f - 1)
                        for s, w in ((0, weights(g)), (1, weights(u))):
                            for k in range(KD):
                                ins = mm(proj[f % 2][:, s * T:(s + 1) * T], w[:, k, i * P:(i + 1) * P], hnT[:, k, :],
                                         start=(k == 0), stop=(k == KD - 1))
                        ff_mm.by(ins)
                        if former:
                            down_tile(*former)
                        former = (f, d, i)
                    release(g, ff_mm)
                    release(u, ff_mm)
                down_tile(*former)

            def routing():
                for t in range(NT):
                    for k in range(KD):
                        ins = mm(B[4][:, NE * t:NE * t + NE], hnT[:, k, t * P:(t + 1) * P], router_w[:, k, :],
                                 start=(k == 0), stop=(k == KD - 1))
                ins.then_inc(logit_mm, 1)
                pe.wait_ge(oneh_ready, 1)
                oh = [rt[:, t, 0, :] for t in range(NT)]
                mm(B[5][:, 0:NE], before[:], oh[0], start=True, stop=True)
                mm(B[5][:, NE:2 * NE], before[:], oh[1], start=True, stop=False)
                mm(B[5][:, NE:2 * NE], ones[:], oh[0], start=False, stop=True)
                mm(B[5][:, 2 * NE:3 * NE], ones[:], oh[0], start=True, stop=False)
                mm(B[5][:, 2 * NE:3 * NE], ones[:], oh[1], start=False, stop=True).then_inc(rank_mm, 1)

            def gather(i):
                pe.wait_ge(sel_ready, i + 1)
                for k in range(KD):
                    cs = slice((k % 4) * CAP, (k % 4 + 1) * CAP)
                    mm(B[k // 4][:, cs], hn[:, 0, k * P:(k + 1) * P], sel[:, 0, :], start=True, stop=False)
                    ins = mm(B[k // 4][:, cs], hn[:, 1, k * P:(k + 1) * P], sel[:, 1, :], start=False, stop=True)
                    if k % 4 == 3:
                        ins.then_inc(gather_mm, 1)

            def experts():
                pe.wait_ge(passes_ready, 1)
                n_pass = pe.value_load(pass_expert[0:1, 0:1], min_val=1, max_val=MAX_PASSES)
                gather(0)
                with pe.Fori(0, n_pass) as i:

                    def arrived_load(k):
                        pe.wait_ge(slot_loaded[k % MRING], i * 48 + 16 * (slot_count[k % MRING] + k // MRING + 1))

                    def down_tile(f):
                        pe.wait_ge(he_ready, i * FT + (f + 1))
                        n = 3 * (f // 2) + 2
                        if f % 2 == 0:
                            arrived_load(n)
                        w = slot(n % MRING).rearrange("p (k n) -> p k n", k=2)
                        for half in range(2):
                            ins = mm(B[4 + half][0:CAP, :], heT[:, f, :], w[:, f % 2, half * 512:half * 512 + 512],
                                     start=(f == 0), stop=(f == FT - 1), skip_group_check=True)
                        if f % 2:
                            ins.then_inc(down_mm.handle, 1)

                    for f in range(FT):
                        if f % 2 == 0:
                            arrived_load(3 * (f // 2))
                            arrived_load(3 * (f // 2) + 1)
                        if f == 0:
                            pe.wait_ge(xg_ready, i * 2 + 2)
                        else:
                            pe.wait_ge(he_ready, i * FT + (f - 1))
                        for s in range(2):
                            w = slot((3 * (f // 2) + s) % MRING).rearrange("p (k n) -> p k n", k=KD)
                            for k in range(KD):
                                ins = mm(proj[f % 2][:, s * CAP:(s + 1) * CAP], w[:, k, (f % 2) * P:(f % 2 + 1) * P],
                                         xgT[:, k, :], start=(k == 0), stop=(k == KD - 1))
                        ins.then_inc(proj_mm.handle, 1)
                        if f:
                            down_tile(f - 1)
                        if f == 8:
                            pe.wait_ge(sc_added, i * 4 + 4)
                            for t in range(NT):
                                ins = pe.transpose(B[2][0:CAP, t * P:(t + 1) * P], selw[:, t, :], ident[:])
                            ins.then_inc(selT_mm, 1)
                    down_tile(FT - 1)
                    pe.wait_ge(selT_ready, i + 1)
                    gather(i + 1)
                    for half in range(2):
                        pe.wait_ge(ye_ready, i * 2 + (half + 1))
                        pe.wait_ge(xg_ready, i * 2 + 4)
                        for t in range(NT):
                            ins = mm(B[half + 2 * t][:, :], selwT[0:CAP, t * P:(t + 1) * P],
                                     ye[0:CAP, half * 512:half * 512 + 512], start=True, stop=True)
                            ins.then_inc(sc_mm, 1)

            pe.wait_ge(consts_ready, 1)
            pe.wait_ge(vec_loaded, 16 * 11 * DEPTH)
            for l in range(DEPTH):
                ins = pe.transpose(B[5][:, P * l:P * l + V_ROWS], vec_rows[0:V_ROWS, l, :], ident[0:V_ROWS, 0:V_ROWS])
            ins.then_inc(vec_mm, 1)
            for l in range(DEPTH):
                transposes_of_hn(l, 0)
                hnT_ready.wait(pe, l, 4)
                if l == 0:
                    pe.wait_ge(vec_ready, 1)
                    pe.wait_ge(par_loaded, 16 * (6 * DEPTH + 1))
                deltanet(l)
                rwkv(l)
                attention(l)
                merge(l)
                xo_ready.wait(pe, l, 4)
                transposes_of_hn(l, 1)
                hnT_ready.wait(pe, l, 8)
                if l == 0:
                    dense_ffn(l)
                else:
                    routing()
                    experts()

        @block.scalar
        def _(act):
            steps = [0]

            def link(ins):
                steps[0] += 1
                ins.then_inc(act_step, 1)
                act.wait_ge(act_step, steps[0])

            A = act.activation

            def rms(l, half):
                if half == 1:
                    xo_ready.wait(act, l, 4)
                elif l == 0:
                    act.wait_ge(x_loaded, 32)
                else:
                    fx_ready.wait(act, 0, 1)
                for t in range(NT):
                    ins = A(hn[:, t, :], x[:, t, :], ACT.Square, accum_out=stat[:, 32 + t:33 + t])
                link(ins)
                link(A(stat[:, 34:36], stat[:, 32:34], ACT.Ln, scale=1.0 / D, bias=eps_c[:, 0:1]))
                rms_ready.by(A(stat[:, 36:38], stat[:, 34:36], ACT.Exp, scale=-0.5))

            def stage_raw(l, first, n, i0):
                for i in range(n):
                    proj_mm.wait(act, l, first + i + 1)
                    if i0 + i >= 2:
                        raw_used.wait(act, l, i0 + i - 1)
                    raw_ready.by(A(stage[:, (i0 + i) % 2, :, 4:260],
                                   proj_view(l, first + i), ACT.Copy))

            def proj_view(l, i):
                return proj[(l * proj_mm.per_layer + i) % 2][:, :].rearrange("p (s t) -> p s t", s=2)

            def solver(l, run):
                for g in range(2):
                    x0_mm.wait(act, l, 2 * run + g + 1)
                    x0_ready.by(A(X[:, 4 * g:4 * g + 4, :], B[2 + g][:, :].rearrange("p (i n) -> p i n", i=4), ACT.Copy))
                for b in range(1, 6):
                    for g in range(2):
                        n = 10 * run + 2 * (b - 1) + g
                        y_mm.wait(act, l, n + 1)
                        y_ready.by(A(Y[:, 4 * g:4 * g + 4, :], B[g][:, :].rearrange("p (i n) -> p i n", i=4), ACT.Copy))

            def deltanet(l):
                stage_raw(l, 0, 6, 0)
                for i in range(3):
                    raw_used.wait(act, l, 2 * i + 2)
                    qkv_silu.by(A(qkv[:, 4 * i:4 * i + 4, :], qkv[:, 4 * i:4 * i + 4, :], ACT.Silu))
                for i in range(2):
                    proj_mm.wait(act, l, 6 + i + 1)
                    zt_ready.by(A(zT[:, 2 * i:2 * i + 2, :], proj_view(l, 6 + i), ACT.Silu))
                qkv_silu.wait(act, l, 2)
                square_ready.by(A(square[:, :, :], qkv[:, 0:8, :], ACT.Square))
                A(stat[:, 60:64], head_scalars[:, l, 0, :], ACT.Exp)
                ba_abs.wait(act, l, 1)
                link(A(sc[:, 16:32], sc[:, 16:32], ACT.Exp, scale=-1.0))
                ba_ln.by(A(sc[:, 16:32], sc[:, 16:32], ACT.Ln, bias=1.0))
                stats_mm.wait(act, l, 1)
                A(sc[:, 64:80], B[5][:, 48:64], ACT.Exp)
                lnr_ready.by(A(sc[:, 48:64], B[5][:, 16:32], ACT.Ln, bias=eps_c[:, 1:2]))
                scal_ready.wait(act, l, 1)
                A(sc[:, 120:128], sc[:, 80:88], ACT.Exp)
                expo_scal.by(A(sc[:, 128:144], sc[:, 104:120], ACT.Exp))
                for t in range(NT):
                    for k in range(2):
                        n = 2 * t + k
                        if k == 1:
                            bcast_mm.wait(act, l, n + 1)
                            qfac_ready.by(A(U[:, t], B[5][:, :].rearrange("p (h n) -> p h n", h=GH), ACT.Exp))
                        expo_ready.wait(act, l, n + 1)
                        for h in range(GH):
                            ins = A(EE[:, t, k, h, :], EE[:, t, k, h, :], ACT.Exp,
                                    bias=sc[:, 96 + 4 * t + h:97 + 4 * t + h])
                        decay_ready.by(ins)
                solver(l, 0)
                for t in range(NT):
                    uw_mm.wait(act, l, t + 1)
                    if t == 0:
                        qdec_ready.wait(act, l, 2)
                    uw_ready.by(A(U[:, t], B[t][:, :].rearrange("p (h n) -> p h n", h=GH), ACT.Copy))
                for t in range(NT):
                    uw_mm.wait(act, l, 2 + t + 1)
                    uw_ready.by(A(wT[:, t], B[2 + t][:, :].rearrange("p (h n) -> p h n", h=GH), ACT.Copy, scale=-1.0))
                for t in range(NT):
                    o_mm.wait(act, l, t + 1)
                    osq_ready.by(A(on[:, t], B[t][:, :].rearrange("p (h n) -> p h n", h=GH), ACT.Square))
                    oss_ready.wait(act, l, t + 1)
                    link(A(stat[:, 44 + 4 * t:48 + 4 * t], stat[:, 44 + 4 * t:48 + 4 * t], ACT.Ln, scale=1.0 / P,
                           bias=eps_c[:, 0:1]))
                    ors_ready.by(A(stat[:, 44 + 4 * t:48 + 4 * t], stat[:, 44 + 4 * t:48 + 4 * t], ACT.Exp, scale=-0.5))

            def rwkv(l):
                stage_raw(l, 8, 7, 6)
                raw_used.wait(act, l, 13)
                lora_in.by(A(hl[0:64, 12, :], hl[0:64, 12, :], ACT.Tanh))
                lora_in.by(A(hl[:, 13, :], hl[:, 13, :], ACT.Sigmoid))
                for q in range(2):
                    a_mm.wait(act, l, q + 1)
                    for s in range(2):
                        j = 2 * q + s
                        ins = A(aT[:, j, :], B[2 + q][:, s * T:(s + 1) * T], ACT.Sigmoid,
                                bias=vecs[:, l, V_A0 + j:V_A0 + j + 1])
                a_ready.by(ins)
                u_ready.wait(act, l, 2)
                lw_ready.by(A(lw[:, :, :], lw[:, :, :], ACT.Sigmoid))
                for q in range(2):
                    kk2_mm.wait(act, l, q + 1)
                    if q == 0:
                        kk2_mm.wait(act, l, 2)
                    ins = A(rsq[:, 2 * q:2 * q + 2, :], B[4 + q][:, :].rearrange("p (s t) -> p s t", s=2), ACT.Ln,
                            bias=eps_c[:, 1:2])
                link(ins)
                krs_ready.by(A(rsq[:, :, :], rsq[:, :, :], ACT.Exp, scale=-0.5))
                for q in range(2):
                    for t in range(NT):
                        for j in range(2):
                            n = 4 * q + 2 * t + j
                            bank = B[2 * t + j]
                            L_mm.wait(act, l, n + 1)
                            if t == 0 and j == 0 and q:
                                z_ready.wait(act, l, 4)
                            A(E[:, t, j, 0:2, :], bank[:, 0:2 * P].rearrange("p (k n) -> p k n", k=2), ACT.Exp)
                            A(E[:, t, j, 2, :], bank[:, 0:P], ACT.Exp, scale=-1.0)
                            E_ready.by(A(Ec[:, t, j, :], bank[:, 2 * P:2 * P + 4], ACT.Exp))
                    krbk_ready.wait(act, l, 4 * q + 4)
                    for t in range(NT):
                        for k in range(2):
                            bank = (B[4], B[5], B[0], B[1])[2 * t + k]
                            tk_mm.wait(act, l, 4 * q + 2 * t + k + 1)
                            if k == 0:
                                A(TK[:, t, 0, :], bank[:, 0:T], ACT.Copy)
                                tk_ready.by(A(TK[:, t, 1, :], bank[:, T:2 * T], ACT.Copy, scale=-1.0))
                            else:
                                tk_ready.by(A(TK[:, t, 2:4, :], bank[:, :].rearrange("p (k n) -> p k n", k=2), ACT.Copy))
                    solver(l, 1 + q)
                    av_mm.wait(act, l, q + 1)
                    av_ready.by(A(Av[:, :, :, :], B[0][:, :].rearrange("p (t j n) -> p t j n", t=NT, j=2), ACT.Copy))
                    rw_mm.wait(act, l, 2 * q + 1)
                    rw_ready.by(A(WcT[:, :, :, :], B[2][:, :].rearrange("p (t j n) -> p t j n", t=NT, j=2), ACT.Copy))
                    rw_mm.wait(act, l, 2 * q + 2)
                    rw_ready.by(A(RU[:, :, :, :], B[1][:, :].rearrange("p (t j n) -> p t j n", t=NT, j=2), ACT.Copy))
                    for t in range(NT):
                        ry_mm.wait(act, l, 2 * q + t + 1)
                        ry_ready.by(A(y_tok[:, t, q * T:(q + 1) * T], (B[5], B[0])[t][:, 0:T], ACT.Copy))
                ysum_ready.wait(act, l, 1)
                ysq_ready.by(A(ysq[:, :, :], y_tok[:, :, :], ACT.Square))
                yvar_ready.wait(act, l, 1)
                link(A(sc[:, 160:176], sc[:, 160:176], ACT.Ln, scale=1.0 / 64, bias=eps_c[:, 2:3]))
                yrs_ready.by(A(sc[:, 160:176], sc[:, 160:176], ACT.Exp, scale=-0.5))

            def attention(l):
                ob_ready.wait(act, l, 2)
                for i in range(4):
                    proj_mm.wait(act, l, 15 + i + 1)
                    qk_ready.by(A(qkT[:, 2 * i:2 * i + 2, :], proj_view(l, 15 + i), ACT.Copy,
                                  scale=0.125 if i < 2 else 1.0))
                for t in range(NT):
                    proj_mm.wait(act, l, 19 + t + 1)
                    sv_ready.by(A(sv[:, t, :], proj[(l * proj_mm.per_layer + 19 + t) % 2][:, :], ACT.Copy))

                def log1p(h):
                    z_scores.wait(act, l, h + 1)
                    if h >= 2:
                        sp_raw.wait(act, l, h - 1)
                    link(A(absz[:, h % 2, :], B[h % 4][:, 0:384], ACT.Abs))
                    link(A(absz[:, h % 2, :], absz[:, h % 2, :], ACT.Exp, scale=-1.0))
                    l1_ready.by(A(absz[:, h % 2, :], absz[:, h % 2, :], ACT.Ln, bias=1.0))

                log1p(0)
                for h in range(8):
                    if h < 7:
                        log1p(h + 1)
                    loga_mm.wait(act, l, h + 1)
                    if h >= 2:
                        pv_mm.wait(act, l, h - 1)
                    att_raw.by(A(att[:, h % 2, :], B[h % 4][:, 0:384], ACT.Exp))
                    if h % 2:
                        j = h // 2
                        pv_mm.wait(act, l, h + 1)
                        oc_ready.by(A(oT[:, 2, j, :], B[4 + j % 2][:, 0:T], ACT.Copy))

            def merge(l):
                for m in range(12):
                    proj_mm.wait(act, l, 21 + 2 * m + 1)
                    if m >= 2:
                        merge_step.wait(act, l, m - 1)
                    gate_ready.by(A(gate[:, m % 2, :], proj[(l * proj_mm.per_layer + 21 + 2 * m) % 2][:, :], ACT.Sigmoid))

            def dense_ffn(l):
                for f in range(FFD // P):
                    ff_mm.wait(act, 0, f + 1)
                    if f >= 2:
                        ff_ready.wait(act, 0, f - 1)
                    ff_silu.by(A(sg[:, f % 2, 0:T], proj[f % 2][:, 0:T], ACT.Silu))

            act.wait_ge(consts_ready, 1)
            act.wait_ge(par_loaded, 16 * (6 * DEPTH + 1))
            for l in range(DEPTH):
                rms(l, 0)
                if l == 0:
                    act.wait_ge(vec_ready, 1)
                deltanet(l)
                rwkv(l)
                attention(l)
                merge(l)
                rms(l, 1)
                if l == 0:
                    dense_ffn(l)
            act.wait_ge(margin_ready, 1)
            A(rs[:, 8:10], rs[:, 4:6], ACT.Exp).then_inc(marg_exp, 1)
            act.wait_ge(passes_ready, 1)
            n_pass = act.value_load(pass_expert[0:1, 0:1], min_val=1, max_val=MAX_PASSES)
            with act.Fori(0, n_pass) as i:
                for f in range(FT):
                    act.wait_ge(proj_mm.handle, i * FT + (hid_base + f + 1))
                    if f >= 2:
                        act.wait_ge(he_ready, i * FT + (f - 1))
                    A(sge[:, f % 2, :], proj[f % 2][:, 0:CAP], ACT.Silu).then_inc(he_silu, 1)
                act.wait_ge(down_mm.handle, i * (FT // 2) + (down_base + FT // 2))
                for half in range(2):
                    A(ye[0:CAP, half * 512:half * 512 + 512], B[4 + half][0:CAP, :], ACT.Copy).then_inc(ye_ready, 1)
            act.wait_ge(all_added, 1)
            for t in range(NT):
                ins = A(hn[:, t, :], x[:, t, :], ACT.Square, accum_out=stat[:, 32 + t:33 + t])
            link(ins)
            link(A(stat[:, 34:36], stat[:, 32:34], ACT.Ln, scale=1.0 / D, bias=eps_c[:, 0:1]))
            A(stat[:, 36:38], stat[:, 34:36], ACT.Exp, scale=-0.5).then_inc(frms_ready, 1)

        @block.vector
        def _(v):
            steps = [0]

            def link(ins):
                steps[0] += 1
                ins.then_inc(dve_step, 1)
                v.wait_ge(dve_step, steps[0])

            tt, ts, stt = v.tensor_tensor, v.tensor_scalar, v.scalar_tensor_tensor
            heads = lambda bank: bank.rearrange("p (h n) -> p h n", h=4)

            def vec(l, row, n=1):
                return vecs[:, l, row:row + n]

            def norm(l, half):
                rms_ready.wait(v, l, half + 1)
                for t in range(NT):
                    xnorm_ready.by(ts(hn[:, t, :], x[:, t, :], stat[:, 36 + t:37 + t], None, ALU.mult))
                if l == 0 and half == 0:
                    v.wait_ge(vec_ready, 1)
                for t in range(NT):
                    for q in range(2):
                        hnT_mm.wait(v, l, 4 * half + 2 * t + q + 1)
                        hnT_ready.by(tt(hnT[:, 4 * q:4 * q + 4, t * P:(t + 1) * P], heads(B[2 * t + q][:, :]),
                                        over(vec(l, (V_NMG, V_NFG)[half] + 4 * q, 4), P), ALU.mult))

            def solver(l, run):
                for g in range(2):
                    ml_ready.wait(v, l, 12 * run + g + 1)
                    xt0_ready.by(tt(XT[:, 4 * g:4 * g + 4, :], rep(ident[:], 4), Ml[:, 4 * g:4 * g + 4, :], ALU.subtract))
                for b in range(1, 6):
                    for g in range(2):
                        x_mm.wait(v, l, 10 * run + 2 * (b - 1) + g + 1)
                        gs = slice(4 * g, 4 * g + 4)
                        if b < 5:
                            tt(X[:, gs, :], X[:, gs, :], heads(B[2 + g][:, :]), ALU.subtract)
                        x_ready.by(tt(XT[:, gs, :], XT[:, gs, :], heads(B[4 + g][:, :]), ALU.subtract))

            def deltanet(l):
                link(v.memset(stage[:, :, :, 0:4], 0.0))
                for i in range(6):
                    raw_ready.wait(v, l, i + 1)
                    for tap in range(4):
                        for s in range(2):
                            j = 2 * i + s
                            src = stage[:, i % 2, s, 1 + tap:1 + tap + T]
                            w = vec(l, V_CONV + 12 * tap + j)
                            if tap == 0:
                                ins = ts(qkv[:, j, :], src, w, None, ALU.mult)
                            else:
                                ins = stt(qkv[:, j, :], src, w, qkv[:, j, :], ALU.mult, ALU.add)
                        if tap < 3:
                            link(ins)
                    raw_used.by(ins)
                ba_mm.wait(v, l, 1)
                ba = B[4][:, 0:16].rearrange("p (t n) -> p t n", t=NT)
                w = sc[:, 0:16].rearrange("p (k t h) -> p k t h", k=2, t=NT)
                tt(w[:, 0], ba[:, :, 4:8], rep(head_scalars[:, l, 1, :], NT), ALU.add)
                link(ts(w[:, 1], ba[:, :, 0:4], -1.0, None, ALU.mult))
                ba_abs.by(stt(sc[:, 16:32], sc[:, 0:16], -1.0, sc[:, 0:16], ALU.mult, ALU.max))
                ba_ln.wait(v, l, 1)
                link(stt(sc[:, 32:48], sc[:, 0:16], 0.0, sc[:, 16:32], ALU.max, ALU.add))
                sp3 = sc[:, 32:48].rearrange("p (k t h) -> p k t h", k=2, t=NT)
                g_ready.by(stt(stat[:, 0:8].rearrange("p (t h) -> p t h", t=NT), sp3[:, 0], -1.0,
                               rep(stat[:, 60:64], NT), ALU.mult, ALU.mult))
                lnr_ready.wait(v, l, 1)
                th = lambda lo: sc[:, lo:lo + 8].rearrange("p (t h) -> p t h", t=NT)
                lnq = sc[:, 48:64].rearrange("p (t n) -> p t n", t=NT)[:, :, 0:4]
                lnk = sc[:, 48:64].rearrange("p (t n) -> p t n", t=NT)[:, :, 4:8]
                G = B[5][:, 32:40].rearrange("p (t h) -> p t h", t=NT)
                Gt = B[5][:, 40:48].rearrange("p (t h) -> p t h", t=NT)
                stt(th(80), lnk, -0.5, G, ALU.mult, ALU.add)
                stt(th(88), lnq, -0.5, G, ALU.mult, ALU.add)
                stt(th(96), lnk, -0.5, G, ALU.mult, ALU.subtract)
                link(ts(th(112), sp3[:, 1], -1.0, None, ALU.mult))
                tt(th(80), th(80), th(112), ALU.add)
                ts(th(88), th(88), -0.5 * math.log(P), None, ALU.add)
                link(tt(th(104), th(96), Gt, ALU.add))
                scal_ready.by(v.memset(S[:, :, :], 0.0))
                for t in range(NT):
                    for k in range(2):
                        diag_ready.by(tt(diag[:, t, k], rep(ident[:], GH), over(sc[:, 80 + 8 * k + 4 * t:84 + 8 * k + 4 * t], P),
                                         ALU.mult))
                for t in range(NT):
                    for k in range(2):
                        bcast_mm.wait(v, l, 2 * t + k + 1)
                        if k == 1:
                            qfac_ready.wait(v, l, t + 1)
                        ins = tt(EE[:, t, k], heads(B[4 + k][:, :]), rep((neg_strict, neg_incl)[k][:], GH), ALU.add)
                        expo_ready.by(ins)
                expo_scal.wait(v, l, 1)
                for t in range(NT):
                    kv_mm.wait(v, l, t + 1)
                    tt(kb[:, t], heads(B[t][:, :]), over(sc[:, 120 + 4 * t:124 + 4 * t], P), ALU.mult)
                    kv_read.by(tt(kdec[:, t], heads(B[t][:, :]), over(sc[:, 128 + 4 * t:132 + 4 * t], P), ALU.mult))
                for t in range(NT):
                    kv_mm.wait(v, l, 2 + t + 1)
                    kv_read.by(tt(vb[:, t], heads(B[2 + t][:, :]), over(sc[:, 136 + 4 * t:140 + 4 * t], P), ALU.mult))
                for t in range(NT):
                    qfac_ready.wait(v, l, t + 1)
                    qdec_ready.by(tt(qdec[:, t], qkv[:, 0:4, t * P:(t + 1) * P], U[:, t], ALU.mult))
                for t in range(NT):
                    for k in range(2):
                        gram_mm.wait(v, l, 2 * t + k + 1)
                        decay_ready.wait(v, l, 2 * t + k + 1)
                        gram_read.by(tt(EE[:, t, k], heads(B[2 * t + k][:, :]), EE[:, t, k], ALU.mult))
                solver(l, 0)
                s_ready.by(v.memset(S[:, :, :], 0.0))
                for c in range(NCH):
                    t, b = c // 2, C * (c % 2)
                    rows = slice(b, b + C)
                    vn_mm.wait(v, l, c + 1)
                    uw_ready.wait(v, l, 4)
                    vn_ready.by(tt(VN[rows, t], U[rows, t], heads(B[4][rows, :]), ALU.add))
                    if c < NCH - 1:
                        s_mm.wait(v, l, c + 1)
                        for h in range(GH):
                            ins = stt(S[:, h, :], S[:, h, :], sc[:, 64 + 4 * c + h:65 + 4 * c + h],
                                      B[5][:, h * P:(h + 1) * P], ALU.mult, ALU.add)
                        s_ready.by(ins)
                for t in range(NT):
                    osq_ready.wait(v, l, t + 1)
                    oss_ready.by(v.tensor_reduce(stat[:, 44 + 4 * t:48 + 4 * t], on[:, t], AX_X, ALU.add))
                    ors_ready.wait(v, l, t + 1)
                    on_ready.by(tt(on[:, t], heads(B[t][:, :]), over(stat[:, 44 + 4 * t:48 + 4 * t], P), ALU.mult))
                for t in range(NT):
                    onT_mm.wait(v, l, t + 1)
                    zt_ready.wait(v, l, 2)
                    oa_ready.by(stt(oT[:, 0, :, t * P:(t + 1) * P], heads(B[2 + t][:, :]), vec(l, V_GNG),
                                    zT[:, :, t * P:(t + 1) * P], ALU.mult, ALU.mult))

            def rwkv(l):
                for i in range(7):
                    raw_ready.wait(v, l, 6 + i + 1)
                    b = (6 + i) % 2
                    link(tt(hl[:, 2 * i:2 * i + 2, :], stage[:, b, :, 3:259], stage[:, b, :, 4:260], ALU.subtract))
                    for s in range(2):
                        ins = stt(hl[:, 2 * i + s, :], hl[:, 2 * i + s, :], vec(l, V_MU + 2 * i + s),
                                  stage[:, b, s, 4:260], ALU.mult, ALU.add)
                    raw_used.by(ins)
                r, k, val = hl[:, 0:4, :], hl[:, 4:8, :], hl[:, 8:12, :]
                raw_used.wait(v, l, 13)
                link(tt(kkT[:, :, :], k, over(vec(l, V_KK, 4), T), ALU.mult))
                kk2_ready.by(tt(rsq[:, :, :], kkT[:, :, :], kkT[:, :, :], ALU.mult))
                for t in range(NT):
                    u_mm.wait(v, l, t + 1)
                    u_ready.by(tt(lw[:, t, :], B[t][:, :], w0[:, l, :], ALU.add))
                a_ready.wait(v, l, 1)
                link(stt(rtmp2[:, :, :], aT[:, :, :], -1.0, over(vec(l, V_KA, 4), T), ALU.add, ALU.mult))
                tt(rtmp[:, :, :], r, over(vec(l, V_RK, 4), T), ALU.mult)
                link(stt(k, rtmp2[:, :, :], 1.0, k, ALU.add, ALU.mult))
                rk_ready.by(tt(rtmp[:, :, :], rtmp[:, :, :], k, ALU.mult))
                krs_ready.wait(v, l, 1)
                link(tt(kkT[:, :, :], kkT[:, :, :], rsq[:, :, :], ALU.mult))
                tt(aT[:, :, :], aT[:, :, :], kkT[:, :, :], ALU.mult)
                for q in range(2):
                    rk_mm.wait(v, l, q + 1)
                    ins = tt(bonus[:, 2 * q:2 * q + 2, :], B[q][:, :].rearrange("p (s t) -> p s t", s=2),
                             hl[:, 8 + 2 * q:10 + 2 * q, :], ALU.mult)
                feat_ready.by(ins)
                feat_ready.wait(v, l, 1)
                for q in range(2):
                    for t in range(NT):
                        for j in range(2):
                            E_ready.wait(v, l, 4 * q + 2 * t + j + 1)
                            p, ds = 2 * q + j, slice(t * P, (t + 1) * P)
                            tt(KR[:, t, j, 0, :], kkT[:, p, ds], E[:, t, j, 1, :], ALU.mult)
                            tt(KR[:, t, j, 1, :], hl[:, p, ds], E[:, t, j, 0, :], ALU.mult)
                            tt(BK[:, t, j, 0, :], aT[:, p, ds], E[:, t, j, 2, :], ALU.mult)
                            krbk_ready.by(tt(BK[:, t, j, 1, :], hl[:, 4 + p, ds], E[:, t, j, 2, :], ALU.mult))
                    for c in range(NCH - 1):
                        ins = tt(Dc[:, :, c], Ec[:, c // 2, :, c % 2], Ec[:, (c + 1) // 2, :, 2 + (c + 1) % 2], ALU.mult)
                    if q:
                        ry_mm.wait(v, l, 2)
                    v.memset(Z[:, 0, :, :], 0.0)
                    v.memset(Z[:, 1, :, :], 0.0)
                    v.memset(Z[:, 2, :, :], 0.0)
                    z_ready.by(v.memset(Z[:, 3, :, :], 0.0))
                    for i in range(8):
                        n = 8 * q + i
                        g4_mm.wait(v, l, n + 1)
                        g4_ready.by(tt(G4[:, i], heads(B[2 + i % 2][:, :]), gram_mask[:, :, :], ALU.mult))
                    solver(l, 1 + q)
                    for c in range(NCH):
                        t, b = c // 2, C * (c % 2)
                        rows = slice(b, b + C)
                        n = 4 * q + c
                        c_mm.wait(v, l, n + 1)
                        rw_ready.wait(v, l, 2 * q + 2)
                        c_ready.by(tt(RC[rows, t], RU[rows, t], B[3][rows, 0:T].rearrange("p (j n) -> p j n", j=2), ALU.add))
                        if c < NCH - 1:
                            z_mm.wait(v, l, 3 * q + c + 1)
                            for e in range(2):
                                rs_, cs = slice(64 * e, 64 * e + 64), slice(64 * e, 64 * e + 64)
                                zb = B[4][rs_, 0:T].rearrange("p (j n) -> p j n", j=2)[:, :, cs]
                                ins = tt(Z[rs_, c + 1, :, cs], Z[rs_, c, :, cs], zb, ALU.add)
                            link(ins)
                            for e in range(2):
                                rs_, cs = slice(64 * e, 64 * e + 64), slice(64 * e, 64 * e + 64)
                                ins = tt(Z[rs_, c + 1, :, cs], Z[rs_, c + 1, :, cs], over(Dc[rs_, :, c], 64), ALU.mult)
                            z_ready.by(ins)
                ry_ready.wait(v, l, 4)
                y3 = y_tok[:, :, :].rearrange("p t (h n) -> p (t h) n", h=8)
                link(v.tensor_reduce(sc[:, 144:160], y3, AX_X, ALU.add))
                link(ts(sc[:, 144:160], sc[:, 144:160], 1.0 / 64, None, ALU.mult))
                ysum_ready.by(tt(y3, y3, over(sc[:, 144:160], 64), ALU.subtract))
                ysq_ready.wait(v, l, 1)
                yvar_ready.by(v.tensor_reduce(sc[:, 160:176], ysq[:, :, :].rearrange("p t (h n) -> p (t h) n", h=8), AX_X,
                                              ALU.add))
                yrs_ready.wait(v, l, 1)
                yn_ready.by(tt(y3, y3, over(sc[:, 160:176], 64), ALU.mult))
                for t in range(NT):
                    ynT_mm.wait(v, l, t + 1)
                    for j in range(RP):
                        ins = ts(rtmp[:, j, t * P:(t + 1) * P], B[1 + t][:, j * P:(j + 1) * P], vec(l, V_LNG + j),
                                 vec(l, V_LNB + j), ALU.mult, ALU.add)
                link(ins)
                link(tt(rtmp[:, :, :], rtmp[:, :, :], bonus[:, :, :], ALU.add))
                for q in range(2):
                    rgate_mm.wait(v, l, q + 1)
                    ob_ready.by(tt(oT[:, 1, 2 * q:2 * q + 2, :], rtmp[:, 2 * q:2 * q + 2, :],
                                   B[3 + q][:, :].rearrange("p (s t) -> p s t", s=2), ALU.mult))

            def attention(l):
                for h in range(8):
                    l1_ready.wait(v, l, h + 1)
                    if h >= 2:
                        loga_mm.wait(v, l, h - 1)
                    sp_raw.by(stt(sp[:, h % 2, :], B[h % 4][:, 0:384], 0.0, absz[:, h % 2, :], ALU.max, ALU.add))

            def merge(l):
                for m in range(12):
                    jj = (m % 4) * 2
                    gate_ready.wait(v, l, m + 1)
                    proj_mm.wait(v, l, 22 + 2 * m + 1)
                    bank = proj[(l * proj_mm.per_layer + 22 + 2 * m) % 2][:, :].rearrange("p (s t) -> p s t", s=2)
                    g = gate[:, m % 2, :].rearrange("p (s t) -> p s t", s=2)
                    if m < 4:
                        merge_step.by(tt(mT[:, jj:jj + 2, :], bank, g, ALU.mult))
                    else:
                        mt3 = mtmp.rearrange("p (s t) -> p s t", s=2)
                        link(tt(mt3, bank, g, ALU.mult))
                        merge_step.by(tt(mT[:, jj:jj + 2, :], mT[:, jj:jj + 2, :], mt3, ALU.add))
                for half in range(2):
                    for t in range(NT):
                        xo_mm.wait(v, l, 2 * half + t + 1)
                        cs = slice(512 * half, 512 * half + 512)
                        xo_ready.by(tt(x[:, t, cs], x[:, t, cs], B[2 * half + t][:, :], ALU.add))

            def dense_ffn(l):
                for f in range(FFD // P):
                    ff_silu.wait(v, 0, f + 1)
                    ff_ready.by(tt(ffT[:, f, :], sg[:, f % 2, 0:T], proj[f % 2][:, T:2 * T], ALU.mult))
                down_mm.wait(v, 0, down_mm.per_layer)
                for t in range(NT):
                    for half in range(2):
                        cs = slice(512 * half, 512 * half + 512)
                        ins = tt(x[:, t, cs], x[:, t, cs], B[2 * t + half][:, :], ALU.add)
                fx_ready.by(ins)
                fx_ready.wait(v, 0, 1)

            def routing():
                V = lambda k: rt[:, :, k, :]
                col = lambda k: rs[:, 2 * k:2 * k + 2]
                for t in range(NT):
                    link(ts(rt[:, t, 9, :], slots_iota[:, 0:NE], -1.0, float(NE), ALU.mult, ALU.add))
                v.wait_ge(logit_mm, 1)
                link(v.tensor_copy(V(1), B[4][:, 0:2 * NE].rearrange("p (t e) -> p t e", t=NT)))

                def first_of_greatest(src, mx, onehot):
                    link(v.tensor_reduce(mx, src, AX_X, ALU.max))
                    link(tt(V(2), src, over(mx, NE), ALU.is_equal))
                    link(tt(V(2), V(2), V(9), ALU.mult))
                    link(v.tensor_reduce(col(3), V(2), AX_X, ALU.max))
                    link(tt(onehot, V(9), over(col(3), NE), ALU.is_equal))

                first_of_greatest(V(1), col(0), V(3))
                link(stt(V(4), V(3), NEG, V(1), ALU.mult, ALU.add))
                first_of_greatest(V(4), col(1), V(5))
                tt(col(2), col(1), col(0), ALU.subtract).then_inc(margin_ready, 1)
                tt(V(0), V(3), V(5), ALU.add).then_inc(oneh_ready, 1)
                v.wait_ge(marg_exp, 1)
                link(ts(col(5), col(4), 1.0, None, ALU.add))
                link(v.reciprocal(col(6), col(5)))
                link(tt(col(7), col(4), col(6), ALU.mult))
                v.wait_ge(rank_mm, 1)
                total = B[5][:, 2 * NE:3 * NE]
                link(ts(rt[:, 0, 6, :], total, 0.5, None, ALU.is_ge))
                for n in range(1, -(-T // CAP)):
                    link(stt(rt[:, 0, 6, :], total, n * CAP + 0.5, rt[:, 0, 6, :], ALU.is_ge, ALU.add))
                link(v.tensor_copy(rt[:, 0, 7, :], rt[:, 0, 6, :]))
                for e in range(1, NE):
                    link(tt(rt[:, 0, 7, e:e + 1], rt[:, 0, 7, e - 1:e], rt[:, 0, 6, e:e + 1], ALU.add))
                link(tt(rt[:, 0, 8, :], rt[:, 0, 7, :], rt[:, 0, 6, :], ALU.subtract))
                for t in range(NT):
                    link(stt(rt[:, t, 10, :], rt[:, 0, 8, :], float(CAP), B[5][:, NE * t:NE * t + NE], ALU.mult, ALU.add))
                for k, onehot in ((8, V(3)), (9, V(5))):
                    link(tt(V(2), onehot, V(10), ALU.mult))
                    link(v.tensor_reduce(col(k), V(2), AX_X, ALU.add))
                for i in range(MAX_PASSES):
                    link(ts(rt[0:1, 0, 11, :], rt[0:1, 0, 7, :], float(i) + 0.5, None, ALU.is_le))
                    link(v.tensor_reduce(table[0:1, i + 1:i + 2], rt[0:1, 0, 11, :], AX_X, ALU.add))
                link(v.tensor_copy(table[0:1, 0:1], rt[0:1, 0, 7, NE - 1:NE]))
                link(ts(table[0:1, 1:MAX_PASSES + 1], table[0:1, 1:MAX_PASSES + 1], float(NE - 1), None, ALU.min))
                v.tensor_copy(pass_expert[0:1, 0:MAX_PASSES + 1], table[0:1, 0:MAX_PASSES + 1]).then_inc(passes_ready, 1)
                v.wait_ge(passes_ready, 1)

            def places(i):
                for t in range(NT):
                    p1, p2 = rs[:, 16 + t:17 + t], rs[:, 18 + t:19 + t]
                    w1, w2 = rs[:, 12 + t:13 + t], rs[:, 14 + t:15 + t]
                    ts(sel[:, t, :], slots_iota[:], p1, None, ALU.is_equal)
                    ts(selw[:, t, :], slots_iota[:], p1, w1, ALU.is_equal, ALU.mult)
                    ts(selb[:, t, :], slots_iota[:], p2, w2, ALU.is_equal, ALU.mult).then_inc(seld, 1)
                    v.wait_ge(seld, i * 4 + (2 * t + 1))
                    stt(sel[:, t, :], slots_iota[:], p2, sel[:, t, :], ALU.is_equal, ALU.add)
                    ins = tt(selw[:, t, :], selw[:, t, :], selb[:, t, :], ALU.add)
                    if t == 0:
                        ins.then_inc(seld, 1)
                ins.then_inc(sel_ready, 1)
                v.wait_ge(sel_ready, i + 1)
                ts(rs[:, 16:20], rs[:, 16:20], -float(CAP), None, ALU.add).then_inc(seld, 1)
                v.wait_ge(seld, i * 4 + 4)

            def gathered(i):
                for q in range(2):
                    v.wait_ge(gather_mm, i * 2 + (q + 1))
                    tt(xgT[:, 4 * q:4 * q + 4, :], B[q][:, 0:4 * CAP].rearrange("p (k n) -> p k n", k=4),
                       over(vec(1, V_NFG + 4 * q, 4), CAP), ALU.mult).then_inc(xg_ready, 1)

            def experts():
                n_pass = v.value_load(pass_expert[0:1, 0:1], min_val=1, max_val=MAX_PASSES)
                v.memset(rs[:, 61:62], 0.0).then_inc(sc_added, 4)
                places(0)
                gathered(0)
                with v.Fori(0, n_pass) as i:
                    for f in range(FT):
                        v.wait_ge(he_silu, i * FT + (f + 1))
                        tt(heT[:, f, :], sge[:, f % 2, :], proj[f % 2][:, CAP:2 * CAP], ALU.mult).then_inc(he_ready, 1)
                        if f == 9:
                            v.wait_ge(selT_mm, i + 1)
                            v.tensor_copy(selwT[0:CAP, :], B[2][0:CAP, 0:T]).then_inc(selT_ready, 1)
                            places(i + 1)
                    gathered(i + 1)
                    for half in range(2):
                        for t in range(NT):
                            v.wait_ge(sc_mm, i * 4 + (2 * half + t + 1))
                            cs = slice(half * 512, half * 512 + 512)
                            ins = tt(x[:, t, cs], x[:, t, cs], B[half + 2 * t][:, :], ALU.add)
                            ins.then_inc(sc_added, 1)

            v.wait_ge(vec_mm, 1)
            v.tensor_copy(vecs[:, :, 0:V_ROWS], B[5][:, 0:2 * P].rearrange("p (l n) -> p l n", l=DEPTH)[:, :, 0:V_ROWS]
                          ).then_inc(vec_ready, 1)
            v.wait_ge(consts_ready, 1)
            v.wait_ge(par_loaded, 16 * (6 * DEPTH + 1))
            for l in range(DEPTH):
                norm(l, 0)
                deltanet(l)
                rwkv(l)
                attention(l)
                merge(l)
                norm(l, 1)
                if l == 0:
                    dense_ffn(l)
            routing()
            experts()
            v.memset(rs[:, 60:61], 0.0).then_inc(all_added, 1)
            v.wait_ge(frms_ready, 1)
            v.wait_ge(fgain_loaded, 16)
            for t in range(NT):
                stt(x[:, t, :], x[:, t, :], stat[:, 36 + t:37 + t], fgain, ALU.mult, ALU.mult).then_inc(fin_ready, 1)

        @block.sync
        def _(sp_):
            for t in range(NT):
                sp_.dma_start(x[:, t, :], a["x"][0, t * P:(t + 1) * P, :]).then_inc(x_loaded, 16)
            for l in range(DEPTH):
                for name, row, n in (("norm_mix_g", V_NMG, 8), ("norm_ffn_g", V_NFG, 8), ("rwkv_mu", V_MU, 14),
                                     ("rwkv_a0", V_A0, 4), ("rwkv_k_k", V_KK, 4), ("rwkv_k_a", V_KA, 4),
                                     ("rwkv_ln_g", V_LNG, 4), ("rwkv_ln_b", V_LNB, 4), ("gdn_norm_g", V_GNG, 1)):
                    sp_.dma_start(vec_rows[row:row + n, l, :],
                                  a[name][l].rearrange("(r n) -> r n", n=P)).then_inc(vec_loaded, 16)
                sp_.dma_start(vec_rows[V_RK:V_RK + 4, l, :],
                              a["rwkv_r_k"][l].rearrange("(r h) n -> r (h n)", h=2)).then_inc(vec_loaded, 16)
                sp_.dma_start(vec_rows[V_CONV:V_CONV + 48, l, :],
                              a["gdn_conv_w"][l].rearrange("i (r n) -> (i r) n", n=P)).then_inc(vec_loaded, 16)

            def load(n):
                src, _, s, _, former = loads[n]
                if former is not None:
                    sp_.wait_ge(*freed[former])
                if n == L[0]["ffn_first"]:
                    xo_ready.wait(sp_, 0, 4)
                sp_.dma_start(weights(n), src).then_inc(slot_loaded[s], 16)

            for n in range(RING):
                load(n)
            for l in range(DEPTH):
                sp_.dma_start(lora[0:64, l, :], a["rwkv_w2"][l]).then_inc(par_loaded, 16)
                sp_.dma_start(lora[64:128, l, :], a["rwkv_a2"][l]).then_inc(par_loaded, 16)
                sp_.dma_start(g2[:, l, :], a["rwkv_g2"][l]).then_inc(par_loaded, 16)
                sp_.dma_start(w0[:, l, :], a["rwkv_w0"][l].partition_broadcast(P)).then_inc(par_loaded, 16)
                sp_.dma_start(head_scalars[:, l, 0, :], a["gdn_a_log"][l].partition_broadcast(P)).then_inc(par_loaded, 16)
                sp_.dma_start(head_scalars[:, l, 1, :], a["gdn_dt_bias"][l].partition_broadcast(P)).then_inc(par_loaded, 16)
            sp_.dma_start(router_w[:], a["router_w"][0].rearrange("(k p) n -> p k n", p=P)).then_inc(par_loaded, 16)
            for n in range(RING, n_loads):
                load(n)

            for n in slot_last:
                sp_.wait_ge(*freed[n])
            xo_ready.wait(sp_, DEPTH - 1, 4)
            sp_.wait_ge(passes_ready, 1)
            sp_.dma_start(fgain, a["final_norm_g"].partition_broadcast(P)).then_inc(fgain_loaded, 16)
            n_pass = sp_.value_load(pass_expert[0:1, 0:1], min_val=1, max_val=MAX_PASSES)
            with sp_.Fori(0, n_pass) as i:
                e = sp_.value_load(pass_expert[0:1, bass.ds(i + 1, 1)], min_val=0, max_val=NE - 1)
                for k in range(3 * FT // 2):
                    f, kind = k // 3, k % 3
                    pf, pk = divmod(k - MRING, 3)
                    if pk < 2:
                        sp_.wait_ge(proj_mm.handle, i * FT + (hid_base + 2 * pf + 2))
                    else:
                        sp_.wait_ge(down_mm.handle, i * (FT // 2) + (down_base + pf + 1))
                    if kind < 2:
                        w = a["moe_w_gate"] if kind == 0 else a["moe_w_up"]
                        src = w[0, bass.ds(e, 1), :, SW * f:SW * f + SW].rearrange("a (k p) n -> p (a k) n", p=P)
                        k_ = KD
                    else:
                        src = a["moe_w_down"][0, bass.ds(e, 1), SW * f:SW * f + SW, :].rearrange(
                            "a (k p) n -> p (a k) n", p=P)
                        k_ = SW // P
                    sp_.dma_start(slot(k % MRING).rearrange("p (k n) -> p k n", k=k_), src).then_inc(
                        slot_loaded[k % MRING], 16)
            sp_.wait_ge(fin_ready, 1)
            sp_.dma_start(out[0, 0:P, :], x[:, 0, :]).then_inc(out_stored, 16)
            sp_.wait_ge(fin_ready, 2)
            sp_.dma_start(out[0, P:T, :], x[:, 1, :]).then_inc(out_stored, 16)
            sp_.wait_ge(out_stored, 32)

        for name, s in signals:
            assert s.given == s.per_layer * (1 if s in once else DEPTH), (name, s.given, s.per_layer)


_INS = ['x', 'norm_mix_g', 'w_in', 'gdn_conv_w', 'gdn_a_log', 'gdn_dt_bias', 'gdn_norm_g', 'rwkv_mu', 'rwkv_w0',
        'rwkv_w2', 'rwkv_a0', 'rwkv_a2', 'rwkv_g2', 'rwkv_k_k', 'rwkv_k_a', 'rwkv_r_k', 'rwkv_ln_g', 'rwkv_ln_b',
        'w_branch_gdn', 'w_branch_rwkv', 'w_branch_sb', 'w_out', 'norm_ffn_g', 'ffn_w_gate', 'ffn_w_up', 'ffn_w_down',
        'router_w', 'moe_w_gate', 'moe_w_up', 'moe_w_down', 'final_norm_g']


def kernel(**inputs):
    import numpy as _np
    import concourse.bacc as _bacc
    from concourse import mybir as _mybir
    from concourse.bass_utils import run_bass_kernel_spmd as _run

    nc = _bacc.Bacc("TRN2", target_bir_lowering=False, num_devices=1)
    arrays, args = {}, {}
    for name in _INS:
        arr = _np.ascontiguousarray(inputs[name])
        arrays[f"in_{name}_dram"] = arr
        args[name] = nc.dram_tensor(f"in_{name}_dram", arr.shape, _mybir.dt.from_np(arr.dtype), kind="ExternalInput").ap()
    out = nc.dram_tensor("out_0_dram", (1, T, D), F32, kind="ExternalOutput").ap()
    build(nc, args, out)
    r = _run(nc, [arrays], core_ids=[0])
    return r.results[0]["out_0_dram"]
```
